# Optimizing a Trainium2 kernel written in Bass

```python
import jax, jax.numpy as jnp
from jax import lax
import numpy as np

D_MODEL = 1024
BATCH = 1
SEQ = 512
DEPTH = 1

ATT_HEADS = 8
ATT_HEAD_DIM = 64
MOBA_BLOCK = 256
MOBA_TOPK = 3
MOBA_Q_CHUNK = 128
DN_HEADS = 8
DN_HEAD_DIM = 64
DN_CHUNK = 64
CONV_WIDTH = 4
D_FF = 4 * D_MODEL
NORM_EPS = 1e-6

ATT_W = ATT_HEADS * ATT_HEAD_DIM
DN_W = DN_HEADS * DN_HEAD_DIM
IN_SPLITS = (ATT_W, ATT_W, ATT_W, 3 * DN_W, DN_W, DN_HEADS, DN_HEADS, D_MODEL, D_MODEL)
IN_COLS = sum(IN_SPLITS)

kernel_name = "hybrid_moba_gdn_sqrelu_block"

def rms_norm(x, w):
    xf = x.astype(jnp.float32)
    y = xf * lax.rsqrt(jnp.mean(xf * xf, axis=-1, keepdims=True) + NORM_EPS)
    return (y * w.astype(jnp.float32)).astype(x.dtype)

def l2_norm(x):
    xf = x.astype(jnp.float32)
    return xf * lax.rsqrt(jnp.sum(xf * xf, axis=-1, keepdims=True) + NORM_EPS)

def causal_depthwise_conv(x, w):
    c = x.shape[-1]
    return lax.conv_general_dilated(
        x, w[:, None, :].astype(x.dtype), window_strides=(1,),
        padding=[(CONV_WIDTH - 1, 0)], dimension_numbers=("NWC", "WIO", "NWC"),
        feature_group_count=c)

def moba_attention(q, k, v):
    bsz, seq, h, d = q.shape
    nb = -(-seq // MOBA_BLOCK)
    n_sel = min(MOBA_TOPK, nb)
    nc = seq // MOBA_Q_CHUNK
    pad = nb * MOBA_BLOCK - seq
    scale = d ** -0.5
    neg = jnp.finfo(jnp.float32).min

    qh = q.transpose(0, 2, 1, 3)
    kb = jnp.pad(k.transpose(0, 2, 1, 3), ((0, 0), (0, 0), (0, pad), (0, 0)))
    vb = jnp.pad(v.transpose(0, 2, 1, 3), ((0, 0), (0, 0), (0, pad), (0, 0)))
    kb = kb.reshape(bsz, h, nb, MOBA_BLOCK, d)
    vb = vb.reshape(bsz, h, nb, MOBA_BLOCK, d)

    k_mean = jnp.mean(kb.astype(jnp.float32), axis=3)
    pos = jnp.arange(seq)
    blk_scores = jnp.einsum("bhsd,bhnd->bhsn", qh.astype(jnp.float32), k_mean)
    past = jnp.arange(nb)[None, :] < (pos // MOBA_BLOCK)[:, None]
    blk_scores = jnp.where(past, blk_scores, neg)
    _, sel_idx = lax.top_k(blk_scores, n_sel)

    def per_batch(args):
        q_b, kb_b, vb_b, idx_b = args
        q_c = q_b.reshape(h, nc, MOBA_Q_CHUNK, d).transpose(1, 0, 2, 3)
        idx_c = idx_b.reshape(h, nc, MOBA_Q_CHUNK, n_sel).transpose(1, 0, 2, 3)

        def per_chunk(cargs):
            c, qq, ii = cargs
            qpos = c * MOBA_Q_CHUNK + jnp.arange(MOBA_Q_CHUNK)
            own = (c * MOBA_Q_CHUNK) // MOBA_BLOCK
            k_sel = jax.vmap(lambda a, i: a[i])(kb_b, ii)
            v_sel = jax.vmap(lambda a, i: a[i])(vb_b, ii)
            s_sel = jnp.einsum("hcd,hcnkd->hcnk", qq, k_sel).astype(jnp.float32) * scale
            valid = jnp.arange(n_sel)[None, :] < (qpos // MOBA_BLOCK)[:, None]
            s_sel = jnp.where(valid[None, :, :, None], s_sel, neg)
            k_own = lax.dynamic_index_in_dim(kb_b, own, axis=1, keepdims=False)
            v_own = lax.dynamic_index_in_dim(vb_b, own, axis=1, keepdims=False)
            s_own = jnp.einsum("hcd,hkd->hck", qq, k_own).astype(jnp.float32) * scale
            kpos = own * MOBA_BLOCK + jnp.arange(MOBA_BLOCK)
            s_own = jnp.where(kpos[None, :] <= qpos[:, None], s_own, neg)
            scores = jnp.concatenate([s_sel.reshape(h, MOBA_Q_CHUNK, n_sel * MOBA_BLOCK), s_own], axis=-1)
            p = jax.nn.softmax(scores, axis=-1).astype(qq.dtype)
            p_sel = p[..., : n_sel * MOBA_BLOCK].reshape(h, MOBA_Q_CHUNK, n_sel, MOBA_BLOCK)
            p_own = p[..., n_sel * MOBA_BLOCK:]
            return (jnp.einsum("hcnk,hcnkd->hcd", p_sel, v_sel)
                    + jnp.einsum("hck,hkd->hcd", p_own, v_own))

        out = lax.map(per_chunk, (jnp.arange(nc), q_c, idx_c))
        return out.transpose(1, 0, 2, 3).reshape(h, seq, d)

    out = lax.map(per_batch, (qh, kb, vb, sel_idx))
    return out.transpose(0, 2, 1, 3).reshape(bsz, seq, h * d)

def gated_delta_rule(q, k, v, g, beta):
    bsz, seq, h, dk = q.shape
    dv = v.shape[-1]
    n = seq // DN_CHUNK
    f32 = jnp.float32

    def chunks(x):
        x = jnp.moveaxis(x.astype(f32), 2, 1)
        return x.reshape((bsz, h, n, DN_CHUNK) + x.shape[3:])

    qc = chunks(l2_norm(q)) * (dk ** -0.5)
    kc = chunks(l2_norm(k))
    vc = chunks(v)
    bc = chunks(beta)
    gc = jnp.cumsum(chunks(g), axis=-1)

    tri = jnp.tril(jnp.ones((DN_CHUNK, DN_CHUNK), bool))
    strict = jnp.tril(jnp.ones((DN_CHUNK, DN_CHUNK), bool), -1)
    diff = gc[..., :, None] - gc[..., None, :]
    decay = jnp.where(tri, jnp.exp(jnp.where(tri, diff, 0.0)), 0.0)

    k_beta = kc * bc[..., None]
    lower = jnp.where(strict, jnp.einsum("bhnid,bhnjd->bhnij", k_beta, kc) * decay, 0.0)
    a_mat = jnp.eye(DN_CHUNK, dtype=f32) + lower
    rhs = jnp.concatenate([vc * bc[..., None], k_beta * jnp.exp(gc)[..., None]], axis=-1)
    sol = lax.linalg.triangular_solve(a_mat, rhs, left_side=True, lower=True)
    u, w = sol[..., :dv], sol[..., dv:]

    qk = jnp.where(tri, jnp.einsum("bhnid,bhnjd->bhnij", qc, kc) * decay, 0.0)
    q_dec = qc * jnp.exp(gc)[..., None]
    k_dec = kc * jnp.exp(gc[..., -1:] - gc)[..., None]
    g_last = jnp.exp(gc[..., -1])

    def step(state, xs):
        q_i, k_i, u_i, w_i, qk_i, gl_i = xs
        v_new = u_i - jnp.einsum("bhck,bhkv->bhcv", w_i, state)
        o = jnp.einsum("bhck,bhkv->bhcv", q_i, state) + jnp.einsum("bhij,bhjv->bhiv", qk_i, v_new)
        state = state * gl_i[..., None, None] + jnp.einsum("bhck,bhcv->bhkv", k_i, v_new)
        return state, o

    xs = (jnp.moveaxis(q_dec, 2, 0), jnp.moveaxis(k_dec, 2, 0), jnp.moveaxis(u, 2, 0),
          jnp.moveaxis(w, 2, 0), jnp.moveaxis(qk, 2, 0), jnp.moveaxis(g_last, 2, 0))
    state0 = jnp.zeros((bsz, h, dk, dv), f32)
    _, o = lax.scan(step, state0, xs)
    o = jnp.moveaxis(o, 0, 2).reshape(bsz, h, seq, dv)
    return jnp.moveaxis(o, 1, 2)

def hybrid_mixer(h, w_in, conv_w, a_log, dt_bias, dn_norm, w_branch_att, w_branch_dn, w_out):
    bsz, seq, _ = h.shape
    proj = h @ w_in
    split_at = [int(s) for s in np.cumsum(IN_SPLITS)[:-1]]
    qa, ka, va, qkv_dn, z_dn, b_dn, a_dn, gate_att, gate_dn = jnp.split(proj, split_at, axis=-1)

    shp_a = (bsz, seq, ATT_HEADS, ATT_HEAD_DIM)
    y_att = moba_attention(qa.reshape(shp_a), ka.reshape(shp_a), va.reshape(shp_a))

    qkv_dn = jax.nn.silu(causal_depthwise_conv(qkv_dn, conv_w))
    qd, kd, vd = jnp.split(qkv_dn, [DN_W, 2 * DN_W], axis=-1)
    shp_b = (bsz, seq, DN_HEADS, DN_HEAD_DIM)
    beta = jax.nn.sigmoid(b_dn.astype(jnp.float32))
    g = -jnp.exp(a_log.astype(jnp.float32)) * jax.nn.softplus(
        a_dn.astype(jnp.float32) + dt_bias.astype(jnp.float32))
    o_dn = gated_delta_rule(qd.reshape(shp_b), kd.reshape(shp_b), vd.reshape(shp_b), g, beta)
    o_dn = rms_norm(o_dn, dn_norm) * jax.nn.silu(z_dn.reshape(shp_b).astype(jnp.float32))
    y_dn = o_dn.reshape(bsz, seq, DN_W).astype(h.dtype)

    merged = (jax.nn.sigmoid(gate_att) * (y_att @ w_branch_att)
              + jax.nn.sigmoid(gate_dn) * (y_dn @ w_branch_dn))
    return merged @ w_out

def setup_inputs(seed: int = 0) -> dict:
    key = jax.random.key(seed)
    ks = jax.random.split(key, 16)
    f32 = jnp.float32

    def dense(k, fan_in, fan_out):
        return jax.random.normal(k, (DEPTH, fan_in, fan_out), f32) * fan_in ** -0.5

    def gain(k, n):
        return 1.0 + 0.05 * jax.random.normal(k, (DEPTH, n), f32)

    dt = jnp.exp(jax.random.uniform(ks[5], (DEPTH, DN_HEADS), f32, np.log(1e-3), np.log(1e-1)))
    return {
        "x": jax.random.normal(ks[0], (BATCH, SEQ, D_MODEL), f32),
        "pre_norm_mix": gain(ks[1], D_MODEL),
        "w_in": dense(ks[2], D_MODEL, IN_COLS),
        "conv_w": jax.random.normal(ks[3], (DEPTH, CONV_WIDTH, 3 * DN_W), f32) * CONV_WIDTH ** -0.5,
        "a_log": jnp.log(jax.random.uniform(ks[4], (DEPTH, DN_HEADS), f32, 1.0, 16.0)),
        "dt_bias": jnp.log(jnp.expm1(dt)),
        "dn_norm": gain(ks[6], DN_HEAD_DIM),
        "w_branch_att": dense(ks[7], ATT_W, D_MODEL),
        "w_branch_dn": dense(ks[8], DN_W, D_MODEL),
        "w_out": dense(ks[9], D_MODEL, D_MODEL),
        "post_norm_mix": gain(ks[10], D_MODEL),
        "pre_norm_mlp": gain(ks[11], D_MODEL),
        "w_mlp_in": dense(ks[12], D_MODEL, D_FF),
        "w_mlp_out": dense(ks[13], D_FF, D_MODEL),
        "post_norm_mlp": gain(ks[14], D_MODEL),
    }

def reference(x, pre_norm_mix, w_in, conv_w, a_log, dt_bias, dn_norm, w_branch_att, w_branch_dn,
              w_out, post_norm_mix, pre_norm_mlp, w_mlp_in, w_mlp_out, post_norm_mlp):
    for l in range(DEPTH):
        h = rms_norm(x, pre_norm_mix[l])
        y = hybrid_mixer(h, w_in[l], conv_w[l], a_log[l], dt_bias[l], dn_norm[l],
                         w_branch_att[l], w_branch_dn[l], w_out[l])
        x = x + rms_norm(y, post_norm_mix[l])
        h = rms_norm(x, pre_norm_mlp[l])
        y = jnp.square(jax.nn.relu(h @ w_mlp_in[l])) @ w_mlp_out[l]
        x = x + rms_norm(y, post_norm_mlp[l])
    return x


_drawn_inputs = setup_inputs


def setup_inputs(seed=0):
    import zlib

    import numpy as np

    out = dict(_drawn_inputs(seed))
    spreads = {}
    factors = {}
    for name, (base, spread) in spreads.items():
        noise = np.random.default_rng([zlib.crc32(name.encode()), seed]).standard_normal(out[name].shape)
        drawn = base * np.exp(spread * noise) if base else spread * noise
        out[name] = __import__('jax').numpy.asarray(drawn.astype(out[name].dtype))
    for name, factor in factors.items():
        out[name] = (out[name] * factor).astype(out[name].dtype)
    return out
```

```python
from contextlib import ExitStack

import concourse.bass as bass
from concourse import mybir

F32 = mybir.dt.float32
F32R = mybir.dt.float32r
ALU = mybir.AluOpType
ACT = mybir.ActivationFunctionType
AX = mybir.AxisListType

P = 128
D = 1024
S = 512
NT = S // P
KD = D // P
H = 8
HD = 64
W = H * HD
FF = 4 * D
EPS = 1e-6
COL_QK, COL_V, COL_DN, COL_Z, COL_BA, COL_GATE = 0, 2 * W, 3 * W, 6 * W, 7 * W, 7 * W + 2 * H
MASKED = -3.0e38
B32 = 32

RAW = 4
SPL = 4
LEAD = 3
GROUPS = ([(COL_DN + 256 * g, "f") for g in range(6)] + [(COL_QK + 256 * g, "f") for g in range(4)]
          + [(COL_Z, "t"), (COL_V, "t")] + [(COL_GATE + 256 * g, "f") for g in range(8)])


def group_table():
    first, copies, last, out = 0, 0, [0] * 4, []
    turn = 0
    for col, kind in GROUPS:
        if kind == "f":
            banks, n = [turn, turn + 1], 4
            turn = (turn + 2) % 4
        else:
            banks, n = [0, 1, 2, 3], 8
            turn = 0
        need = max(last[b] for b in banks)
        for b in banks:
            copies += 1
            last[b] = copies
        out.append((first, banks, copies, need))
        first += n
    return out


TABLE = group_table()
U_IN = 88
U_BR = U_IN + 16
U_OUT = U_BR + 16
U_M1 = U_OUT + 64
U_ALL = U_M1 + 64
UNIT_GROUP = {}
for _g, (_f, _b, _c, _n) in enumerate(TABLE):
    for _u in range(_f, _f + (4 if GROUPS[_g][1] == "f" else 8)):
        UNIT_GROUP[_u] = _g

ROWS = [(1, 7), (7, 11), (11, 14), (14, 17), (17, 19), (19, 21), (21, 23), (23, 25), (25, 27), (27, 29), (29, 30), (30, 32)]


def side_steps():
    s = [(0, "ba", 0), (2, "bt", 0), (4, "gm", 0)]
    for m in range(12):
        s += [(4 + 4 * (m // 2) + 2 * (m % 2), "cv", m), (6 + 4 * (m // 2) + 2 * (m % 2), "sg", m)]
    for t in range(NT):
        s += [((25, 27, 30, 32)[t], "gk", t), (21 + 2 * t, "ta", t), (29 + 2 * t, "dec", t), (25 + 2 * t, "tb", t),
              (31 + 2 * t, "gr", t), (32 + 2 * t, "qt", t), (39 + 2 * t, "tv", t)]
    for g in range(6, len(GROUPS)):
        n = 4 if GROUPS[g][1] == "f" else 8
        s.append((TABLE[g][0] + n, "ev", g))
    s += [(49 + t, "zz", t) for t in range(NT)]
    s += [(39 + j, "bi", j) for j in range(len(ROWS))] + [(39 + len(ROWS), "bo", 0)]
    for t in range(NT):
        b = 52 + 6 * t
        s += [(b, "ex", t), (b + 2, "lg", t), (b + 3, "lv", t), (b + 3, "lt", t), (b + 4, "l6", t), (b + 5, "l7", t),
              (b + 5, "kk", t), (b + 6, "uw", t), (b + 7, "sa", t), (b + 8, "sb", t), (b + 9, "on", t),
              (b + 10, "oo", t), (b + 11, "op", t), (b + 12, "ot", t)]
    s += [(84, "yp", 0), (85, "yp", 1)]
    for n in range(16):
        s += [(53 + 2 * n, "a1", n), (54 + 2 * n, "an", n), (55 + 2 * n, "a2", n), (57 + 2 * n, "a3", n)]
    rank = {"ev": 0, "an": 1, "uw": 2, "ot": 2, "a3": 3, "a2": 4, "a1": 20}
    return sorted(s, key=lambda x: (min(x[0], U_IN), x[0] if x[0] > U_IN else 0, rank.get(x[1], 9)))


STEPS = side_steps()
BANKS_OF = {"ba": 1, "bt": 1, "gm": 1, "dec": 2, "ta": 2, "tv": 1, "tb": 2, "gr": 4, "qt": 2, "lg": 2, "lv": 2,
            "lt": 2, "l6": 1, "l7": 1, "uw": 2, "sa": 2, "sb": 2, "ot": 1, "a1": 2, "a2": 2, "a3": 1}


def fills():
    out, f = {}, KD
    for _, name, i in STEPS:
        out[name, i] = f
        f += BANKS_OF.get(name, 0)
    return out, f


FILL, FILLS = fills()


def steps_at(unit):
    return [(name, i) for u, name, i in STEPS if min(u, U_IN) == unit]


def program(nc, x, pre_norm_mix, w_in, conv_w, a_log, dt_bias, dn_norm, w_branch_att, w_branch_dn, w_out,
            post_norm_mix, pre_norm_mlp, w_mlp_in, w_mlp_out, post_norm_mlp, out):
    ctx = ExitStack()
    base = (nc.sbuf_base + 63) // 64 * 64
    KB = 1024

    def at(name, kb, shape, dt=F32):
        return nc.alloc_sbuf_tensor_at(name, shape, dt, offset=base + int(kb * KB))

    h_hi = at("h_hi", 0, [P, KD, S], F32R)
    h_lo = at("h_lo", 16, [P, KD, S], F32R)
    raw = at("raw", 32, [P, RAW, 512])
    w_hi = at("w_hi", 40, [P, SPL, 512], F32R)
    w_lo = at("w_lo", 48, [P, SPL, 512], F32R)
    x_sb = at("x_sb", 56, [P, NT, D])
    gate_a = at("gate_a", 56, [P, KD, S])
    qk_dn = at("qk_dn", 72, [P, 8, S])
    t_blocks = at("t_blocks", 80, [P, 32, B32])
    v_blocks = at("v_blocks", 84, [P, 32, B32])
    v_dn = at("v_dn", 88, [P, 4, S])
    v_att = at("v_att", 88, [P, NT, W])
    k_hat = at("k_hat", 96, [P, NT, W])
    beta_v = at("beta_v", 104, [P, NT, W])
    neg_l = at("neg_l", 112, [P, 32, P])
    gate_d = at("gate_d", 112, [P, KD, S])
    qk_t = at("qk_t", 128, [P, 32, P])
    xn = at("xn", 128, [P, NT, D])
    z_sb = at("z_sb", 144, [P, NT, W])
    conv_in = at("conv_in", 152, [P, 2, 3 + S])
    decay1 = at("decay1", 144, [P, H, P])
    qk_m = at("qk_m", 148, [P, H, P])
    l_rows = at("l_rows", 152, [P, B32, B32])
    t_rows = at("t_rows", 156, [P, B32, B32])
    t_bd = at("t_bd", 152, [P, H, P])
    v_bd = at("v_bd", 156, [P, H, P])
    sig = at("sig", 160, [P, 2, S])
    g_mask = at("g_mask", 64, [P, 2, H, P])
    decay0 = at("decay0", 164, [P, H, P])
    probs = at("probs", 160, [P, 2, S])
    probs_t = at("probs_t", 164, [P, 2, S])
    junk = at("junk", 168, [P, D])
    q_tok = at("q_tok", 56, [P, NT, W])
    sq_tok = at("sq_tok", 170, [P, W])
    prod = at("prod", 168, [P, B32 * B32])
    gs = at("gs", 168, [P, H, P])
    u_sb = at("u_sb", 172, [P, W])
    w_t = at("w_t", 174, [P, 4, P])
    state = at("state", 176, [P, 4, P])
    qk_att = at("qk_att", 178, [P, 8, S])
    v_new = at("v_new", 194, [P, W])
    o_acc = at("o_acc", 196, [P, W])
    y_hi = at("y_hi", 128, [P, 8, S], F32R)
    y_lo = at("y_lo", 144, [P, 8, S], F32R)
    m_a = at("m_a", 160, [P, 2, S])
    m_d = at("m_d", 164, [P, 2, S])
    x_res = at("x_res", 96, [P, NT, D])
    pn_mix = at("pn_mix", 80, [P, D])
    pn_mlp = at("pn_mlp", 84, [P, D])
    junk2 = at("junk2", 88, [P, D])
    tmp2 = at("tmp2", 92, [P, D])
    hn = at("hn", 56, [P, NT, D])
    act = at("act", 112, [P, FF // P, S])
    a_hi = at("a_hi", 176, [P, 4, S], F32R)
    a_lo = at("a_lo", 184, [P, 4, S], F32R)
    relu = at("relu", 56, [P, 4, S])
    y_out = at("y_out", 56, [P, NT, D])
    off = [198 * KB]

    def small(name, shape, dt=F32):
        n = 4
        for d in shape[1:]:
            n *= d
        t = nc.alloc_sbuf_tensor_at(name, shape, dt, offset=base + off[0])
        off[0] += (n + 31) // 32 * 32
        return t

    ident = small("ident", [P, P])
    le = small("le", [P, P])
    gt = small("gt", [P, P])
    neg = small("neg", [P, P])
    ones = small("ones", [P, P])
    m32 = small("m32", [P, P])
    own_block = small("own_block", [P, 4])
    wpre = small("wpre", [P, KD])
    wmlp = small("wmlp", [P, KD])
    cw = small("cw", [P, 12, 4])
    dnw = small("dnw", [P, HD])
    dtb = small("dtb", [P, H])
    alog = small("alog", [P, H])
    nhalf = small("nhalf", [P, 16])
    ss = small("ss", [P, 16])
    rs = small("rs", [P, 16])
    ba_raw = small("ba_raw", [P, KD, 16])
    ba_hi = small("ba_hi", [P, KD, 16], F32R)
    ba_lo = small("ba_lo", [P, KD, 16], F32R)
    ba_tok = small("ba_tok", [P, NT, 16])
    beta = small("beta", [P, 32])
    nbeta = small("nbeta", [P, 32])
    g_sb = small("g_sb", [P, 32])
    eg = small("eg", [P, 96])
    be = small("be", [P, 32])
    sp = small("sp", [P, 6, 32])
    ssq = small("ssq", [P, NT, 16])
    flag = small("flag", [P, 1])
    rsq = small("rsq", [P, NT, 16])
    sso = small("sso", [P, H])
    rso = small("rso", [P, H])
    nmax = small("nmax", [P, 2])
    nmax8 = small("nmax8", [P, 2])
    psumr = small("psumr", [P, 2])
    pinv = small("pinv", [P, 2])
    ssy = small("ssy", [P, 8])
    ssh = small("ssh", [P, NT])
    ss2 = small("ss2", [P, NT])
    rs1 = small("rs1", [P, NT])
    rs2 = small("rs2", [P, NT])
    assert base + off[0] <= nc.sbuf_usable_end if hasattr(nc, "sbuf_usable_end") else True
    ba_t = o_acc

    bank = [ctx.enter_context(nc.psum_tensor(f"bank{i}", [P, 512], F32)) for i in range(8)]
    side = bank[4:]

    def sem(name):
        return ctx.enter_context(nc.semaphore(name))

    x_in = [sem(f"x_in{t}") for t in range(NT)]
    small_in = sem("small_in")
    ba_in = sem("ba_in")
    raw_in = [sem(f"raw_in{i}") for i in range(RAW)]
    hi_ready = sem("hi_ready")
    lo_ready = sem("lo_ready")
    unit_done = sem("unit_done")
    bank_copied = sem("bank_copied")
    side_full = sem("side_full")
    side_free = [sem(f"side_free{i}") for i in range(4)]
    consts = sem("consts")
    ss_ready = sem("ss_ready")
    rs_ready = sem("rs_ready")
    xn_ready = sem("xn_ready")
    hhi_ready = sem("hhi_ready")
    bahi_ready = sem("bahi_ready")
    balo_ready = sem("balo_ready")
    conv_done = sem("conv_done")
    sig_done = sem("sig_done")
    silu_done = sem("silu_done")
    ba_args = sem("ba_args")
    ba_acts = sem("ba_acts")
    g_ready = sem("g_ready")
    be_ready = sem("be_ready")
    gmask_ready = sem("gmask_ready")
    ssq_ready = sem("ssq_ready")
    rsq_ready = sem("rsq_ready")
    hat_ready = sem("hat_ready")
    blocks_ready = sem("blocks_ready")
    bd_ready = sem("bd_ready")
    kbg_ready = sem("kbg_ready")
    o_ready = sem("o_ready")
    osq_ready = sem("osq_ready")
    sso_ready = sem("sso_ready")
    rso_ready = sem("rso_ready")
    on_ready = sem("on_ready")
    y_ready = sem("y_ready")
    zsig_done = sem("zsig_done")
    z_ready = sem("z_ready")
    max_ready = sem("max_ready")
    p_ready = sem("p_ready")
    yhi_ready = sem("yhi_ready")
    ylo_ready = sem("ylo_ready")
    gates_ready = sem("gates_ready")
    prod_ready = sem("prod_ready")
    m_ready = sem("m_ready")
    mhi_ready = sem("mhi_ready")
    mlo_ready = sem("mlo_ready")
    xr_in = sem("xr_in")
    pn_in = sem("pn_in")
    ssy_ready = sem("ssy_ready")
    rs1_ready = sem("rs1_ready")
    x2_ready = sem("x2_ready")
    ss2_ready = sem("ss2_ready")
    rs2_ready = sem("rs2_ready")
    hn_ready = sem("hn_ready")
    t2_full = sem("t2_full")
    t2_hi = sem("t2_hi")
    t2_lo = sem("t2_lo")
    relu_done = sem("relu_done")
    act_ready = sem("act_ready")
    ahi_ready = sem("ahi_ready")
    alo_ready = sem("alo_ready")
    ssf_ready = sem("ssf_ready")
    ssh_ready = sem("ssh_ready")
    rsf_ready = sem("rsf_ready")
    y_final = sem("y_final")
    stored = sem("stored")
    act_chain = sem("act_chain")
    dve_chain = sem("dve_chain")
    pool_chain = sem("pool_chain")

    w1 = w_in[0]
    xt = x[0].rearrange("(t p) d -> t p d", p=P)
    ot = out[0].rearrange("(t p) d -> t p d", p=P)

    def unit_source(u):
        if u < U_IN:
            g = UNIT_GROUP[u]
            col, kind = GROUPS[g]
            j = u - TABLE[g][0]
            if kind == "f":
                return w1[j * 256:(j + 1) * 256, col:col + 256].rearrange("(k p) c -> p k c", p=P)
            return w1[j * P:(j + 1) * P, col:col + 512]
        if u < U_BR:
            j = u - U_IN
            w = (w_branch_dn, w_branch_att)[j // 2 % 2][0]
            return w[j % 2 * 256:j % 2 * 256 + 256, j // 4 * 256:j // 4 * 256 + 256].rearrange("(k p) c -> p k c", p=P)
        j = u - U_BR
        return w_out[0][j // 2 * P:j // 2 * P + P, j % 2 * 512:j % 2 * 512 + 512]

    def full(eng, f):
        eng.wait_ge(side_full, f + 1)

    def freed(eng, f):
        if f >= 0:
            eng.wait_ge(side_free[f % 4], f // 4 + 1)

    def heads(ap):
        return ap.rearrange("p (h d) -> p h d", d=HD)

    block = ctx.enter_context(nc.Block())

    @block.sync
    def _(sp_):
        for t in range(NT):
            sp_.dma_start(x_sb[:, t, :], xt[t]).then_inc(x_in[t], 16)
        sp_.dma_start(ba_raw[:], w1[:, COL_BA:COL_BA + 16].rearrange("(k p) c -> p k c", p=P)).then_inc(ba_in, 16)

        def load(u, slot, source, used):
            if used is not None:
                sp_.wait_ge(lo_ready, used)
            dst = raw[:, slot, :]
            if len(source.shape) == 3:
                dst = dst.rearrange("p (k c) -> p k c", k=2)
            sp_.dma_start(dst, source).then_inc(raw_in[slot], 16)

        for u in range(U_OUT):
            load(u, u % RAW, unit_source(u), u - RAW + 1 if u >= RAW else None)
            if u == U_IN + 8:
                sp_.wait_ge(ylo_ready, 4)
                sp_.dma_start(x_res[:], x[0].rearrange("(t p) d -> p t d", p=P)).then_inc(xr_in, 16)
                sp_.dma_start(pn_mix[:], post_norm_mix[0].partition_broadcast(P)).then_inc(pn_in, 16)
                sp_.dma_start(pn_mlp[:], post_norm_mlp[0].partition_broadcast(P)).then_inc(pn_in, 16)
        with sp_.Fori(0, 16) as g:
            for j in range(4):
                load(0, j, w_mlp_in[0][j * 256:(j + 1) * 256, bass.ds(g * 256, 256)].rearrange("(k p) c -> p k c", p=P),
                     g * 4 + (U_OUT + j - RAW + 1))
        with sp_.Fori(0, 16) as k2:
            for j in range(4):
                load(0, j, w_mlp_out[0][bass.ds(k2 * 256 + j // 2 * P, P), j % 2 * 512:j % 2 * 512 + 512],
                     k2 * 4 + (U_M1 + j - RAW + 1))
        for t in range(NT):
            sp_.wait_ge(y_final, 2 * t + 2)
            sp_.dma_start(ot[t], y_out[:, t, :]).then_inc(stored, 16)
        sp_.wait_ge(stored, 16 * NT)

    @block.tensor
    def _(pe):
        def three(o, s_hi, s_lo, m_hi, m_lo, start, stop):
            pe.matmul(o, s_hi, m_hi, start=start, stop=False, skip_group_check=True)
            pe.matmul(o, s_hi, m_lo, start=False, stop=False, skip_group_check=True)
            return pe.matmul(o, s_lo, m_hi, start=False, stop=stop, skip_group_check=True)

        def open_fill(f):
            if f >= 4:
                pe.wait_ge(side_free[f % 4], f // 4)
            return side[f % 4]

        pe.wait_ge(consts, 1)
        pe.wait_ge(xn_ready, NT)
        for k in range(KD):
            b = open_fill(k)
            for t in range(NT):
                i = pe.transpose(b[:, t * P:(t + 1) * P], xn[:, t, k * P:(k + 1) * P], ident[:])
            i.then_inc(side_full, 1)
        for k in range(4, 8):
            freed(pe, k)

        def unit(u):
            s = u % SPL
            pe.wait_ge(lo_ready, u + 1)
            if u < U_IN:
                g = UNIT_GROUP[u]
                first, banks, _, need = TABLE[g]
                j = u - first
                if j == 0 and need:
                    pe.wait_ge(bank_copied, need)
                if GROUPS[g][1] == "f":
                    for kk in range(2):
                        k = 2 * j + kk
                        for m in range(2):
                            c = slice(kk * 256 + m * P, kk * 256 + m * P + P)
                            i = three(bank[banks[m]][:], w_hi[:, s, c], w_lo[:, s, c], h_hi[:, k, :], h_lo[:, k, :],
                                      k == 0, k == KD - 1)
                else:
                    for t in range(NT):
                        c = slice(t * P, t * P + P)
                        i = three(bank[t][:], h_hi[:, j, c], h_lo[:, j, c], w_hi[:, s, :], w_lo[:, s, :],
                                  j == 0, j == KD - 1)
            elif u < U_BR:
                g, b, j = (u - U_IN) // 4, (u - U_IN) // 2 % 2, u % 2
                if j == 0 and b == 0:
                    if g == 0:
                        pe.wait_ge(bank_copied, TABLE[-1][2])
                    if g == 1:
                        for f in range(FILLS - 4, FILLS):
                            freed(pe, f)
                    if g >= 2:
                        pe.wait_ge(prod_ready, 4 * (g - 1))
                if g == 0:
                    pe.wait_ge(ylo_ready, 2 * b + j + 1)
                for kk in range(2):
                    k = 2 * j + kk
                    for m in range(2):
                        c = slice(kk * 256 + m * P, kk * 256 + m * P + P)
                        i = three(bank[g % 2 * 4 + b * 2 + m][:], w_hi[:, s, c], w_lo[:, s, c],
                                  y_hi[:, b * 4 + k, :], y_lo[:, b * 4 + k, :], k == 0, k == 3)
            else:
                k, half = (u - U_BR) // 2, u % 2
                if k == 0 and half == 0:
                    pe.wait_ge(prod_ready, 16)
                pe.wait_ge(mlo_ready, k + 1)
                for t in range(NT):
                    c = slice(t * P, t * P + P)
                    i = three(bank[2 * t + half][:], h_hi[:, k, c], h_lo[:, k, c], w_hi[:, s, :], w_lo[:, s, :],
                              k == 0, k == KD - 1)
            i.then_inc(unit_done, 1)

        def side_step(name, i):
            f = FILL[name, i]
            t = i
            tok = slice(t * P, (t + 1) * P) if t < NT else None
            if name == "ba":
                pe.wait_ge(balo_ready, 1)
                b = open_fill(f)
                for k in range(KD):
                    x_ = three(b[0:16, :], ba_hi[:, k, :], ba_lo[:, k, :], h_hi[:, k, :], h_lo[:, k, :], k == 0, k == KD - 1)
                x_.then_inc(side_full, 1)
            elif name == "bt":
                freed(pe, FILL["ba", 0])
                b = open_fill(f)
                for t in range(NT):
                    x_ = pe.transpose(b[:, 16 * t:16 * t + 16], ba_t[0:16, t * P:(t + 1) * P], ident[0:16, 0:16])
                x_.then_inc(side_full, 1)
            elif name == "gm":
                pe.wait_ge(g_ready, 1)
                b = open_fill(f)
                pe.matmul(b[:, 0:32], le[:], g_sb[:], start=True, stop=True)
                pe.matmul(b[:, 32:64], gt[:], g_sb[:], start=True, stop=True)
                pe.matmul(b[:, 64:96], ones[:], g_sb[:], start=True, stop=True).then_inc(side_full, 1)
            elif name == "dec":
                pe.wait_ge(gmask_ready, t + 1)
                for q in range(2):
                    pe.matmul(open_fill(f + q)[:], le[:], g_mask[:, t % 2, 4 * q:4 * q + 4, :], start=True,
                              stop=True).then_inc(side_full, 1)
            elif name in ("ta", "tv"):
                for q, (src, m0) in enumerate(((qk_dn, 0), (qk_dn, 4)) if name == "ta" else ((v_dn, 0),)):
                    pe.wait_ge(silu_done, 8 if name == "ta" else 12)
                    b = open_fill(f + q)
                    for m in range(4):
                        x_ = pe.transpose(b[:, m * P:(m + 1) * P], src[:, m0 + m, tok], ident[:])
                    x_.then_inc(side_full, 1)
            elif name == "tb":
                for q, src in enumerate((k_hat[:, t, :], q_tok[:, t, :])):
                    pe.wait_ge(hat_ready, 2 * t + 1 + q)
                    b = open_fill(f + q)
                    for m in range(4):
                        x_ = pe.transpose(b[:, m * P:(m + 1) * P], src[:, m * P:(m + 1) * P], ident[:])
                    x_.then_inc(side_full, 1)
            elif name == "gr":
                freed(pe, FILL["tb", t])
                freed(pe, FILL["tb", t] + 1)
                for q in range(4):
                    r = slice(q % 2 * HD, q % 2 * HD + HD)
                    b = open_fill(f + q)
                    for pair in range(4):
                        x_ = pe.matmul(b[:, pair * P:(pair + 1) * P], qk_dn[r, (0 if q >= 2 else 4) + pair, tok],
                                       qk_dn[r, 4 + pair, tok], start=True, stop=True)
                    x_.then_inc(side_full, 1)
            elif name == "qt":
                freed(pe, FILL["gr", t] + 3)
                for q in range(2):
                    b = open_fill(f + q)
                    for h in range(4):
                        x_ = pe.transpose(b[:, h * P:(h + 1) * P], qk_m[:, 4 * q + h, :], ident[:])
                    x_.then_inc(side_full, 1)
            elif name in ("lg", "lv", "lt"):
                if name == "lg":
                    pe.wait_ge(bd_ready, 2 * t + 2)
                elif name == "lv":
                    freed(pe, FILL["lg", t])
                    freed(pe, FILL["lg", t] + 1)
                for q in range(2):
                    b = open_fill(f + q)
                    for h in range(4 * q, 4 * q + 4):
                        lhs, rhs = {"lg": (neg_l[:, 8 * t + h, :], v_bd[:, h, :]), "lv": (t_bd[:, h, :], gs[:, h, :]),
                                    "lt": (gs[:, h, :], t_bd[:, h, :])}[name]
                        x_ = pe.matmul(b[:, h % 4 * P:h % 4 * P + P], lhs, rhs, start=True, stop=True)
                    x_.then_inc(side_full, 1)
            elif name == "l6":
                for q in range(2):
                    freed(pe, FILL["lv", t] + q)
                    freed(pe, FILL["lt", t] + q)
                b = open_fill(f)
                for h in range(H):
                    x_ = pe.matmul(b[0:64, h * 64:h * 64 + 64], neg_l[64:128, 8 * t + h, 0:64], v_bd[64:128, h, 64:128],
                                   start=True, stop=True)
                x_.then_inc(side_full, 1)
            elif name == "l7":
                freed(pe, FILL["l6", t])
                b = open_fill(f)
                for h in range(H):
                    x_ = pe.matmul(b[0:64, h * 64:h * 64 + 64], t_bd[0:64, h, 0:64],
                                   gs[0:64, h // 2, h % 2 * 64:h % 2 * 64 + 64], start=True, stop=True)
                x_.then_inc(side_full, 1)
            elif name == "uw":
                freed(pe, FILL["l7", t])
                pe.wait_ge(kbg_ready, t + 1)
                b = open_fill(f)
                for h in range(H):
                    r = slice(h % 2 * HD, h % 2 * HD + HD)
                    x_ = pe.matmul(b[r, h // 2 * P:h // 2 * P + P], u_sb[:, h * HD:(h + 1) * HD], v_bd[:, h, :],
                                   start=True, stop=True)
                x_.then_inc(side_full, 1)
                b = open_fill(f + 1)
                for h in range(H):
                    x_ = pe.matmul(b[:, h * HD:(h + 1) * HD], v_bd[:, h, :], beta_v[:, t, h * HD:(h + 1) * HD],
                                   start=True, stop=True)
                x_.then_inc(side_full, 1)
            elif name == "sa":
                freed(pe, FILL["uw", t])
                if t:
                    freed(pe, FILL["sb", t - 1] + 1)
                for q in range(2):
                    b = open_fill(f + q)
                    for pair in range(4):
                        x_ = pe.matmul(b[:, pair * P:(pair + 1) * P], w_t[:, pair, :] if q == 0 else qk_dn[:, pair, tok],
                                       state[:, pair, :], start=True, stop=True)
                    x_.then_inc(side_full, 1)
            elif name == "sb":
                freed(pe, FILL["sa", t])
                pe.wait_ge(kbg_ready, t + 1)
                freed(pe, FILL["qt", t] + 1)
                b = open_fill(f)
                for h in range(H):
                    hc = slice(h * HD, (h + 1) * HD)
                    x_ = pe.matmul(b[:, hc], qk_t[:, 8 * t + h, :], v_new[:, hc], start=True, stop=True)
                x_.then_inc(side_full, 1)
                b = open_fill(f + 1)
                for h in range(H):
                    hc = slice(h * HD, (h + 1) * HD)
                    r = slice(h % 2 * HD, h % 2 * HD + HD)
                    x_ = pe.matmul(b[r, h // 2 * HD:h // 2 * HD + HD], k_hat[:, t, hc], v_new[:, hc], start=True, stop=True)
                x_.then_inc(side_full, 1)
            elif name == "ot":
                pe.wait_ge(y_ready, t + 1)
                b = open_fill(f)
                for m in range(4):
                    x_ = pe.transpose(b[:, m * P:(m + 1) * P], o_acc[:, m * P:(m + 1) * P], ident[:])
                x_.then_inc(side_full, 1)
            elif name == "a1":
                t, pair = i // 4, i % 4
                pe.wait_ge(bank_copied, TABLE[9][2])
                for hh in range(2):
                    r = slice(hh * HD, hh * HD + HD)
                    pe.matmul(open_fill(f + hh)[:, 0:(t + 1) * P], qk_att[r, pair, t * P:(t + 1) * P],
                              qk_att[r, 4 + pair, 0:(t + 1) * P], start=True, stop=True).then_inc(side_full, 1)
            elif name == "a2":
                t = i // 4
                for hh in range(2):
                    pe.wait_ge(p_ready, 2 * i + 1 + hh)
                    b = open_fill(f + hh)
                    for kt in range(t + 1):
                        x_ = pe.transpose(b[:, kt * P:(kt + 1) * P], probs[:, hh, kt * P:(kt + 1) * P], ident[:])
                    x_.then_inc(side_full, 1)
            elif name == "a3":
                t, pair = i // 4, i % 4
                pe.wait_ge(bank_copied, TABLE[11][2])
                freed(pe, FILL["a2", i])
                freed(pe, FILL["a2", i] + 1)
                b = open_fill(f)
                for hh in range(2):
                    h = 2 * pair + hh
                    for kt in range(t + 1):
                        x_ = pe.matmul(b[hh * HD:hh * HD + HD, 0:P], v_att[:, kt, h * HD:(h + 1) * HD],
                                       probs_t[:, hh, kt * P:(kt + 1) * P], start=kt == 0, stop=kt == t)
                x_.then_inc(side_full, 1)

        for u in range(U_OUT):
            if u < U_IN:
                unit(u)
                for name, i in steps_at(u):
                    side_step(name, i)
            else:
                if u == U_IN:
                    for name, i in steps_at(u):
                        side_step(name, i)
                unit(u)

        for k in range(KD):
            if k == 0:
                pe.wait_ge(hn_ready, NT)
            for t in range(NT):
                i = pe.transpose(bank[k][:, t * P:(t + 1) * P], hn[:, t, k * P:(k + 1) * P], ident[:])
            i.then_inc(t2_full, 1)
        pe.wait_ge(t2_lo, KD)

        def mlp_in(i, first):
            for q in range(2):
                if not first or q > 1:
                    pe.wait_ge(relu_done, i * 4 + (2 * q - 2))
                for j in range(4):
                    pe.wait_ge(lo_ready, i * 8 + (U_OUT + 4 * q + j + 1))
                    for kk in range(2):
                        for m in range(2):
                            c = slice(kk * 256 + m * P, kk * 256 + m * P + P)
                            k = 2 * j + kk
                            x_ = three(bank[2 * q + m][:], w_hi[:, j, c], w_lo[:, j, c], h_hi[:, k, :], h_lo[:, k, :],
                                       k == 0, k == KD - 1)
                    x_.then_inc(unit_done, 1)

        mlp_in(0, True)
        with pe.Fori(1, 8) as i:
            mlp_in(i, False)

        def mlp_out(i, first, last):
            for kt in range(4):
                pe.wait_ge(alo_ready, i * 4 + (kt + 1))
                for half in range(2):
                    j = 2 * kt + half
                    pe.wait_ge(lo_ready, i * 8 + (U_M1 + j + 1))
                    for t in range(NT):
                        c = slice(t * P, t * P + P)
                        x_ = three(bank[2 * t + half][:], a_hi[:, kt, c], a_lo[:, kt, c], w_hi[:, j % 4, :],
                                   w_lo[:, j % 4, :], first and kt == 0, last and kt == 3)
                    x_.then_inc(unit_done, 1)

        pe.wait_ge(relu_done, 32)
        mlp_out(0, True, False)
        with pe.Fori(1, 7) as i:
            mlp_out(i, False, False)
        mlp_out(7, False, True)

    @block.scalar
    def _(a):
        n = {}

        def mark(i, s):
            n[s.name] = n.get(s.name, 0) + 1
            i.then_inc(s, 1)
            a.wait_ge(s, n[s.name])

        def release(i, f):
            i.then_inc(side_free[f % 4], 1)
            a.wait_ge(side_free[f % 4], f // 4 + 1)

        def copy(o, i_, scale=1.0):
            return a.activation(o, i_, ACT.Copy, scale=scale)

        for dst, src in ((wpre, pre_norm_mix), (wmlp, pre_norm_mlp), (cw, conv_w),
                         (dnw, dn_norm[0].partition_broadcast(P)), (dtb, dt_bias[0].partition_broadcast(P)),
                         (alog, a_log[0].partition_broadcast(P))):
            a.dma_start(dst[:], src).then_inc(small_in, 16)
        for t in range(NT):
            a.wait_ge(x_in[t], 16)
            mark(a.activation(junk[:], x_sb[:, t, :], ACT.Square, accum_out=ss[:, t:t + 1]), ss_ready)
        a.wait_ge(small_in, 16 * 6)
        for k in range(KD):
            full(a, k)
            mark(copy(h_hi[:, k, :], side[k % 4][:], wpre[:, k:k + 1]), hhi_ready)

        def split(u, slot, loaded, used):
            a.wait_ge(raw_in[slot], loaded)
            if used is not None:
                a.wait_ge(unit_done, used)
            copy(w_hi[:, slot, :], raw[:, slot, :]).then_inc(hi_ready, 1)

        def split_u(u):
            split(u, u % 4, 16 * (u // 4 + 1), u - 3 if u >= 4 else None)

        a.wait_ge(ba_in, 16)
        mark(copy(ba_hi[:], ba_raw[:]), bahi_ready)
        for u in range(LEAD):
            split_u(u)

        def side_step(name, i):
            f = FILL[name, i]
            t = i
            tok = slice(t * P, (t + 1) * P) if t < NT else None
            if name == "yp":
                if i == 0:
                    a.wait_ge(y_ready, NT)
                y_hi_part(i)
            if name == "ba":
                full(a, f)
                release(copy(ba_t[0:16, :], side[f % 4][0:16, :]), f)
            elif name == "bt":
                a.wait_ge(ba_args, 2)
                mark(a.activation(beta[:].rearrange("p (t h) -> p t h", h=H), ba_tok[:, :, 0:H], ACT.Sigmoid), ba_acts)
                mark(a.activation(sp[:, 2, :], sp[:, 1, :], ACT.Exp), ba_acts)
                mark(a.activation(alog[:], alog[:], ACT.Exp), ba_acts)
            elif name == "gm":
                full(a, f)
                release(a.activation(eg[:], side[f % 4][:, 0:96], ACT.Exp), f)
            elif name == "cv":
                first, banks, copies, _ = TABLE[i // 2]
                a.wait_ge(unit_done, first + 4)
                if i >= 2:
                    a.wait_ge(conv_done, i - 1)
                else:
                    a.wait_ge(consts, 1)
                mark(copy(conv_in[:, i % 2, 3:3 + S], bank[banks[i % 2]][:]), bank_copied)
            elif name == "sg":
                a.wait_ge(conv_done, i + 1)
                if i >= 2:
                    a.wait_ge(silu_done, i - 1)
                src = qk_dn[:, i, :] if i < 8 else v_dn[:, i - 8, :]
                mark(a.activation(sig[:, i % 2, :], src, ACT.Sigmoid), sig_done)
            elif name == "ev":
                first, banks, copies, _ = TABLE[i]
                a.wait_ge(unit_done, first + (4 if GROUPS[i][1] == "f" else 8))
                if i == 16:
                    full(a, FILL["l6", 3])
                for m, b in enumerate(banks):
                    if i < 10:
                        dst = qk_att[:, 2 * (i - 6) + m, :]
                    elif i == 10:
                        dst = z_sb[:, m, :]
                    elif i == 11:
                        dst = v_att[:, m, :]
                    elif i < 16:
                        dst = gate_a[:, 2 * (i - 12) + m, :]
                    else:
                        dst = gate_d[:, 2 * (i - 16) + m, :]
                    mark(copy(dst, bank[b][:]), bank_copied)
            elif name == "dec":
                a.wait_ge(silu_done, 12)
                if t >= 2:
                    freed(a, FILL["gr", t - 2] + 3)
                d = (decay0, decay1)[t % 2]
                for q in range(2):
                    full(a, f + q)
                    release(a.activation(d[:, 4 * q:4 * q + 4, :], side[(f + q) % 4][:].rearrange("p (h j) -> p h j", j=P),
                                         ACT.Exp), f + q)
            elif name == "ta":
                full(a, f)
                release(copy(q_tok[:, t, :], side[f % 4][:]), f)
                full(a, f + 1)
                release(copy(k_hat[:, t, :], side[(f + 1) % 4][:]), f + 1)
            elif name == "tb":
                full(a, f + 1)
                release(copy(qk_dn[:, 0:4, tok], side[(f + 1) % 4][:].rearrange("p (m t) -> p m t", t=P), HD ** -0.5), f + 1)
            elif name == "zz":
                if t >= 2:
                    a.wait_ge(z_ready, t - 1)
                mark(a.activation((u_sb[:] if t % 2 == 0 else w_t[:].rearrange("p a b -> p (a b)")), z_sb[:, t, :],
                                  ACT.Sigmoid), zsig_done)
            elif name == "l6":
                full(a, f)
                release(copy(gs[0:64, 0:4, :], side[f % 4][0:64, :].rearrange("p (h j) -> p h j", j=P)), f)
            elif name == "l7":
                full(a, f)
                release(copy(v_bd[0:64, :, 64:128], side[f % 4][0:64, :].rearrange("p (h j) -> p h j", j=64)), f)
            elif name == "uw":
                full(a, f)
                release(copy(w_t[:], side[f % 4][:].rearrange("p (h j) -> p h j", j=P)), f)
                full(a, f + 1)
                release(copy(u_sb[:], side[(f + 1) % 4][:]), f + 1)
            elif name == "ot":
                full(a, f)
                release(copy(qk_dn[:, 0:4, tok], side[f % 4][:].rearrange("p (m t) -> p m t", t=P)), f)
            elif name == "a1":
                t = i // 4
                for hh in range(2):
                    a.wait_ge(max_ready, 2 * i + 1 + hh)
                    if i and hh == 0:
                        full(a, FILL["a2", i - 1] + 1)
                    release(a.activation(probs[:, hh, 0:(t + 1) * P], side[(f + hh) % 4][:, 0:(t + 1) * P], ACT.Exp,
                                         bias=nmax8[:, hh:hh + 1], scale=HD ** -0.5, accum_out=psumr[:, hh:hh + 1]), f + hh)
            elif name == "a2":
                t = i // 4
                full(a, f)
                if i:
                    full(a, FILL["a3", i - 1])
                release(copy(probs_t[:, 0, 0:(t + 1) * P], side[f % 4][:, 0:(t + 1) * P]), f)

        def y_hi_part(j):
            src = (qk_dn, qk_att)[j // 2]
            mark(copy(y_hi[:, 2 * j:2 * j + 2, :], src[:, 2 * (j % 2):2 * (j % 2) + 2, :]), yhi_ready)

        for u in range(U_IN + 1):
            if u < U_IN:
                split_u(u + LEAD)
            for name, i in steps_at(u):
                side_step(name, i)

        for f in range(FILLS - 4, FILLS):
            freed(a, f)
        y_hi_part(2)
        y_hi_part(3)
        for u in range(U_IN, U_OUT):
            split_u(u + LEAD)
            if u < U_BR and (u - U_IN) % 4 == 0:
                g = (u - U_IN) // 4
                for gt_ in (gate_a, gate_d):
                    mark(a.activation(gt_[:, 2 * g:2 * g + 2, :], gt_[:, 2 * g:2 * g + 2, :], ACT.Sigmoid), gates_ready)
            if u - U_IN in (5, 9, 13, 17):
                g = (u - U_IN - 5) // 4
                for m in range(2):
                    a.wait_ge(m_ready, 2 * g + m + 1)
                    mark(copy(h_hi[:, 2 * g + m, :], m_a[:, m, :]), mhi_ready)

        a.wait_ge(unit_done, U_OUT)
        for t in range(NT):
            for half in range(2):
                b = 2 * t + half
                mark(a.activation(junk2[:, 0:512], bank[b][:], ACT.Square, accum_out=ssy[:, b:b + 1]), ssy_ready)
        for t in range(NT):
            a.wait_ge(x2_ready, 2 * t + 2)
            mark(a.activation(junk2[:], x_res[:, t, :], ACT.Square, accum_out=ss2[:, t:t + 1]), ss2_ready)
        for k in range(KD):
            a.wait_ge(t2_full, k + 1)
            mark(copy(h_hi[:, k, :], bank[k][:], wmlp[:, k:k + 1]), t2_hi)

        def relu_group(i, q, first):
            a.wait_ge(unit_done, i * 8 + (U_OUT + 4 * q + 4))
            for m in range(2):
                if not first:
                    a.wait_ge(act_ready, i * 4 + (2 * q + m + 1 - 4))
                a.activation(relu[:, 2 * q + m, :], bank[2 * q + m][:], ACT.Relu).then_inc(relu_done, 1)

        def mlp_in(i, first):
            for j in range(8):
                u = U_OUT + LEAD + j
                split(None, u % 4, i * 32 + 16 * (u // 4 + 1), i * 8 + (u - 3))
                if j in (3, 7):
                    relu_group(i, j // 4, first)

        mlp_in(0, True)
        with a.Fori(1, 8) as i:
            mlp_in(i, False)

        def act_hi(i, kt, used):
            a.wait_ge(act_ready, i * 4 + (kt + 1) if not isinstance(i, int) else 4 * i + kt + 1)
            if used:
                a.wait_ge(unit_done, i * 8 + (U_M1 + 2 * (kt - 4) + 2))
            copy(a_hi[:, kt % 4, :], act[:, bass.ds(i * 4 + kt, 1), :].rearrange("p a s -> p (a s)")).then_inc(ahi_ready, 1)

        act_hi(0, 0, False)
        act_hi(0, 1, False)

        def mlp_out(i, first, last):
            for j in range(8):
                u = U_M1 + LEAD + j
                if not (last and j >= 8 - LEAD):
                    split(None, u % 4, i * 32 + 16 * (u // 4 + 1), i * 8 + (u - 3))
                if j % 2 == 0 and not (last and j >= 4):
                    act_hi(i, j // 2 + 2, not (first and j < 4))

        mlp_out(0, True, False)
        with a.Fori(1, 7) as i:
            mlp_out(i, False, False)
        mlp_out(7, False, True)
        a.wait_ge(unit_done, U_ALL)
        a.wait_ge(act_chain, 0)
        for t in range(NT):
            for half in range(2):
                b = 2 * t + half
                mark(a.activation(junk2[:, 0:512], bank[b][:], ACT.Square, accum_out=ssy[:, b:b + 1]), ssf_ready)

    @block.vector
    def _(v):
        n = {}

        def mark(i, s):
            n[s.name] = n.get(s.name, 0) + 1
            i.then_inc(s, 1)
            v.wait_ge(s, n[s.name])

        def link(i):
            mark(i, dve_chain)

        def release(i, f):
            i.then_inc(side_free[f % 4], 1)
            v.wait_ge(side_free[f % 4], f // 4 + 1)

        def stt(o, i0, s, i1, op0, op1):
            return v.scalar_tensor_tensor(out=o, in0=i0, scalar=s, in1=i1, op0=op0, op1=op1)

        def per_head(ap):
            return ap.unsqueeze(2).to_broadcast([P, H, HD])

        v.wait_ge(rs_ready, 1)
        for t in range(NT):
            mark(v.tensor_scalar(xn[:, t, :], x_sb[:, t, :], rs[:, t:t + 1], None, ALU.mult), xn_ready)
        v.wait_ge(small_in, 16 * 6)
        for k in range(KD):
            v.wait_ge(hhi_ready, k + 1)
            release(stt(h_lo[:, k, :], side[k % 4][:], wpre[:, k:k + 1], h_hi[:, k, :].bitcast(F32), ALU.mult,
                        ALU.subtract), k)

        def side_step(name, i):
            f = FILL[name, i]
            t = i
            tok = slice(t * P, (t + 1) * P) if t < NT else None
            if name == "yp":
                y_lo_part(i)
            if name == "bt":
                full(v, f)
                b = side[f % 4]
                release(v.tensor_copy(ba_tok[:], b[:, 0:64].rearrange("p (t c) -> p t c", c=16)), f)
                v.wait_ge(small_in, 16 * 6)
                s3 = [sp[:, q, :] for q in range(6)]
                mark(v.tensor_tensor(s3[0].rearrange("p (t h) -> p t h", h=H), ba_tok[:, :, H:2 * H],
                                     dtb[:].unsqueeze(1).to_broadcast([P, NT, H]), ALU.add), ba_args)
                mark(stt(s3[1], s3[0], -1.0, s3[0], ALU.mult, ALU.min), ba_args)
                v.wait_ge(ba_acts, 3)
                link(v.tensor_scalar(s3[3], s3[2], 2.0, None, ALU.add))
                link(v.reciprocal(s3[4], s3[3]))
                link(v.tensor_tensor(s3[1], s3[2], s3[4], ALU.mult))
                link(v.tensor_tensor(s3[2], s3[1], s3[1], ALU.mult))
                link(v.tensor_scalar(s3[3], s3[2], 1.0 / 17, None, ALU.mult))
                for c in (15, 13, 11, 9, 7, 5, 3):
                    link(stt(s3[3], s3[3], 1.0 / c, s3[2], ALU.add, ALU.mult))
                link(stt(s3[4], s3[3], 1.0, s3[1], ALU.add, ALU.mult))
                link(v.tensor_scalar(s3[5], s3[0], 0.0, None, ALU.max))
                link(stt(s3[4], s3[4], 2.0, s3[5], ALU.mult, ALU.add))
                link(v.tensor_scalar(nbeta[:], beta[:], -1.0, None, ALU.mult))
                mark(stt(g_sb[:].rearrange("p (t h) -> p t h", h=H), s3[4].rearrange("p (t h) -> p t h", h=H), -1.0,
                         alog[:].unsqueeze(1).to_broadcast([P, NT, H]), ALU.mult, ALU.mult), g_ready)
            elif name == "gm":
                freed(v, f)
                mark(v.tensor_tensor(be[:], beta[:], eg[:, 0:32], ALU.mult), be_ready)
            elif name == "cv":
                v.wait_ge(bank_copied, i + 1)
                dst = qk_dn[:, i, :] if i < 8 else v_dn[:, i - 8, :]
                c = conv_in[:, i % 2, :]
                link(v.tensor_scalar(dst, c[:, 0:S], cw[:, i, 0:1], None, ALU.mult))
                for j in range(1, 4):
                    x_ = stt(dst, c[:, j:j + S], cw[:, i, j:j + 1], dst, ALU.mult, ALU.add)
                    if j < 3:
                        link(x_)
                mark(x_, conv_done)
            elif name == "ta":
                freed(v, f)
                for q, src in enumerate((q_tok[:, t, :], k_hat[:, t, :])):
                    freed(v, f + q)
                    link(v.tensor_tensor(sq_tok[:], src, src, ALU.mult))
                    x_ = v.tensor_reduce(ssq[:, t, q * H:(q + 1) * H], heads(sq_tok[:]), AX.X, ALU.add)
                    link(x_) if q == 0 else mark(x_, ssq_ready)
            elif name == "tv":
                full(v, f)
                release(v.tensor_tensor(heads(beta_v[:, t, :]), heads(side[f % 4][:]),
                                        per_head(beta[:, t * H:(t + 1) * H]), ALU.mult), f)
            elif name == "tb":
                v.wait_ge(rsq_ready, t + 1)
                for q, src in enumerate((k_hat[:, t, :], q_tok[:, t, :])):
                    mark(v.tensor_tensor(heads(src), heads(src), per_head(rsq[:, t, (1 - q) * H:(2 - q) * H]), ALU.mult), hat_ready)
                full(v, f)
                release(v.tensor_copy(qk_dn[:, 4:8, tok], side[f % 4][:].rearrange("p (m t) -> p m t", t=P)), f)
            elif name == "gr":
                d = (decay0, decay1)[t % 2]
                freed(v, FILL["dec", t])
                freed(v, FILL["dec", t] + 1)
                for q in range(2):
                    full(v, f + q)
                    for pair in range(4):
                        h = 2 * pair + q
                        x_ = stt(neg_l[:, 8 * t + h, :], side[(f + q) % 4][:, pair * P:(pair + 1) * P],
                                 nbeta[:, 8 * t + h:8 * t + h + 1], d[:, h, :], ALU.mult, ALU.mult)
                        if pair < 3:
                            link(x_)
                    release(x_, f + q)
                if t:
                    full(v, FILL["qt", t - 1] + 1)
                for q in range(2):
                    full(v, f + 2 + q)
                    release(v.tensor_tensor(qk_m[:].rearrange("p (a b) j -> p b a j", b=2)[:, q],
                                            side[(f + 2 + q) % 4][:].rearrange("p (a j) -> p a j", j=P),
                                            d[:].rearrange("p (a b) j -> p b a j", b=2)[:, q], ALU.mult), f + 2 + q)
            elif name == "qt":
                for q in range(2):
                    full(v, f + q)
                    release(v.tensor_tensor(qk_t[:, 8 * t + 4 * q:8 * t + 4 * q + 4, :],
                                            side[(f + q) % 4][:].rearrange("p (h i) -> p h i", i=P),
                                            le[:].unsqueeze(1).to_broadcast([P, 4, P]), ALU.mult), f + q)
            elif name == "bi":
                if i == 0:
                    full(v, FILL["qt", 3] + 1)
                    for b in range(4):
                        r = slice(32 * b, 32 * b + 32)
                        link(v.transpose(l_rows[r, :, :], neg_l[r, :, 32 * b:32 * b + 32].rearrange("p u j -> p j u")))
                    link(v.memset(t_rows[:], 0.0))
                    link(v.memset(t_rows[:].rearrange("p a b -> p (a b)")[:, ::33], 1.0))
                for r in range(*ROWS[i]):
                    o = prod[:, 0:r * r].rearrange("p (l j) -> p l j", j=r)
                    link(v.tensor_tensor(o, t_rows[:, 0:r, 0:r].rearrange("p j l -> p l j"),
                                         l_rows[:, 0:r, r].unsqueeze(1).to_broadcast([P, r, r]), ALU.mult))
                    link(v.tensor_reduce(t_rows[:, r, 0:r], o, AX.X, ALU.add))
            elif name == "bo":
                link(v.transpose(t_blocks[:].rearrange("p u l -> p l u"), t_rows[:].rearrange("p i l -> p l i")))
                mark(v.transpose(v_blocks[:].rearrange("p u i -> p i u"), t_rows[:]), blocks_ready)
            elif name == "lg":
                for q in range(2):
                    full(v, f + q)
                    release(v.tensor_tensor(gs[:, 4 * q:4 * q + 4, :], side[(f + q) % 4][:].rearrange("p (h j) -> p h j", j=P),
                                            m32[:].unsqueeze(1).to_broadcast([P, 4, P]), ALU.mult), f + q)
            elif name in ("lv", "lt"):
                m = v_bd if name == "lv" else t_bd
                for q in range(2):
                    full(v, f + q)
                    if name == "lt" and q == 0:
                        full(v, f + 1)
                    release(v.tensor_tensor(m[:, 4 * q:4 * q + 4, :], side[(f + q) % 4][:].rearrange("p (h j) -> p h j", j=P),
                                            m[:, 4 * q:4 * q + 4, :], ALU.add), f + q)
            elif name == "sa":
                freed(v, FILL["uw", t] + 1)
                full(v, f)
                if t:
                    full(v, FILL["ot", t - 1])
                release(v.tensor_tensor(v_new[:], u_sb[:], side[f % 4][:], ALU.subtract), f)
                full(v, f + 1)
                release(v.tensor_tensor(heads(o_acc[:]), heads(side[(f + 1) % 4][:]), per_head(eg[:, t * H:(t + 1) * H]),
                                        ALU.mult), f + 1)
            elif name == "sb":
                full(v, f)
                release(v.tensor_tensor(o_acc[:], side[f % 4][:], o_acc[:], ALU.add), f)
                full(v, f + 1)
                for q in range(2):
                    r = slice(q * HD, q * HD + HD)
                    s_ = state[r, :, r]
                    e_ = eg[r, 64 + t * H + q:64 + (t + 1) * H:2].unsqueeze(2).to_broadcast([HD, 4, HD])
                    link(v.tensor_tensor(s_, s_, e_, ALU.mult))
                    x_ = v.tensor_tensor(s_, side[(f + 1) % 4][r, 0:256].rearrange("p (a d) -> p a d", d=HD), s_, ALU.add)
                    link(x_) if q == 0 else release(x_, f + 1)
                mark(v.memset(flag[:], 0.0), o_ready)
            elif name == "on":
                v.wait_ge(osq_ready, t + 1)
                mark(v.tensor_reduce(sso[:], heads(u_sb[:]), AX.X, ALU.add), sso_ready)
            elif name == "oo":
                v.wait_ge(rso_ready, t + 1)
                mark(v.tensor_tensor(heads(o_acc[:]), heads(o_acc[:]), per_head(rso[:]), ALU.mult), on_ready)
            elif name == "a1":
                t = i // 4
                for hh in range(2):
                    full(v, f + hh)
                    b = side[(f + hh) % 4]
                    link(v.tensor_tensor(b[:, t * P:(t + 1) * P], b[:, t * P:(t + 1) * P], neg[:], ALU.add))
                    if i and hh == 0:
                        freed(v, FILL["a1", i - 1])
                        freed(v, FILL["a1", i - 1] + 1)
                    link(v.tensor_reduce(nmax[:, hh:hh + 1], b[:, 0:(t + 1) * P], AX.X, ALU.max, negate=True))
                    mark(v.tensor_scalar(nmax8[:, hh:hh + 1], nmax[:, hh:hh + 1], HD ** -0.5, None, ALU.mult), max_ready)
            elif name == "an":
                t = i // 4
                for hh in range(2):
                    freed(v, FILL["a1", i] + hh)
                    link(v.reciprocal(pinv[:, hh:hh + 1], psumr[:, hh:hh + 1]))
                    mark(v.tensor_scalar(probs[:, hh, 0:(t + 1) * P], probs[:, hh, 0:(t + 1) * P], pinv[:, hh:hh + 1], None,
                                         ALU.mult), p_ready)
            elif name == "a2":
                t = i // 4
                full(v, f + 1)
                release(v.tensor_copy(probs_t[:, 1, 0:(t + 1) * P], side[(f + 1) % 4][:, 0:(t + 1) * P]), f + 1)
            elif name == "a3":
                t, pair = i // 4, i % 4
                full(v, f)
                release(v.tensor_copy(qk_att[:, pair, t * P:(t + 1) * P], side[f % 4][:, 0:P]), f)

        def y_lo_part(j):
            v.wait_ge(yhi_ready, j + 1)
            src = (qk_dn, qk_att)[j // 2]
            mark(v.tensor_tensor(y_lo[:, 2 * j:2 * j + 2, :], src[:, 2 * (j % 2):2 * (j % 2) + 2, :],
                                 y_hi[:, 2 * j:2 * j + 2, :].bitcast(F32), ALU.subtract), ylo_ready)

        for u in range(U_IN + 1):
            for name, i in steps_at(u):
                side_step(name, i)

        y_lo_part(2)
        y_lo_part(3)
        for g in range(4):
            v.wait_ge(gates_ready, 2 * g + 2)
            v.wait_ge(unit_done, U_IN + 4 * g + 4)
            if g:
                v.wait_ge(mlo_ready, 2 * g)
            for m in range(2):
                for b, (dst, gt_) in enumerate(((m_d, gate_d), (m_a, gate_a))):
                    mark(v.tensor_tensor(dst[:, m, :], bank[g % 2 * 4 + b * 2 + m][:], gt_[:, 2 * g + m, :], ALU.mult),
                         prod_ready)

        v.wait_ge(xr_in, 16)
        v.wait_ge(pn_in, 32)
        for t in range(NT):
            v.wait_ge(ssy_ready, 2 * t + 2)
            mark(v.tensor_tensor(ssh[:, t:t + 1], ssy[:, 2 * t:2 * t + 1], ssy[:, 2 * t + 1:2 * t + 2], ALU.add), ssh_ready)
        for t in range(NT):
            v.wait_ge(rs1_ready, t + 1)
            v.wait_ge(ssy_ready, 8)
            for half in range(2):
                c = slice(half * 512, half * 512 + 512)
                link(stt(tmp2[:, c], bank[2 * t + half][:], rs1[:, t:t + 1], pn_mix[:, c], ALU.mult, ALU.mult))
                mark(v.tensor_tensor(x_res[:, t, c], x_res[:, t, c], tmp2[:, c], ALU.add), x2_ready)
        for t in range(NT):
            v.wait_ge(rs2_ready, t + 1)
            mark(v.tensor_scalar(hn[:, t, :], x_res[:, t, :], rs2[:, t:t + 1], None, ALU.mult), hn_ready)
        for k in range(KD):
            v.wait_ge(t2_hi, k + 1)
            mark(stt(h_lo[:, k, :], bank[k][:], wmlp[:, k:k + 1], h_hi[:, k, :].bitcast(F32), ALU.mult, ALU.subtract), t2_lo)

        def square(i):
            for m in range(4):
                v.wait_ge(relu_done, i * 4 + (m + 1))
                v.tensor_tensor(act[:, bass.ds(i * 4 + m, 1), :].rearrange("p a s -> p (a s)"), relu[:, m, :], relu[:, m, :],
                                ALU.mult).then_inc(act_ready, 1)

        with v.Fori(0, 8) as i:
            square(i)

        def act_lo(i):
            for kt in range(4):
                v.wait_ge(ahi_ready, i * 4 + (kt + 1))
                v.tensor_tensor(a_lo[:, kt, :], act[:, bass.ds(i * 4 + kt, 1), :].rearrange("p a s -> p (a s)"),
                                a_hi[:, kt, :].bitcast(F32), ALU.subtract).then_inc(alo_ready, 1)

        v.wait_ge(act_ready, 32)
        with v.Fori(0, 8) as i:
            act_lo(i)

        for t in range(NT):
            v.wait_ge(ssf_ready, 2 * t + 2)
            mark(v.tensor_tensor(ssh[:, t:t + 1], ssy[:, 2 * t:2 * t + 1], ssy[:, 2 * t + 1:2 * t + 2], ALU.add), ssh_ready)
        for t in range(NT):
            v.wait_ge(rsf_ready, t + 1)
            v.wait_ge(ssf_ready, 8)
            for half in range(2):
                c = slice(half * 512, half * 512 + 512)
                link(stt(tmp2[:, c], bank[2 * t + half][:], rs1[:, t:t + 1], pn_mlp[:, c], ALU.mult, ALU.mult))
                mark(v.tensor_tensor(y_out[:, t, c], x_res[:, t, c], tmp2[:, c], ALU.add), y_final)

    @block.gpsimd
    def _(g):
        n = {}

        def mark(i, s):
            n[s.name] = n.get(s.name, 0) + 1
            i.then_inc(s, 1)
            g.wait_ge(s, n[s.name])

        def link(i):
            mark(i, pool_chain)

        def select(o, op, fill, base_, step, cm):
            return g.affine_select(out=o, in_=o, compare_op=op, fill=fill, base=base_, pattern=[[step, P]],
                                   channel_multiplier=cm)

        for c, val in ((ident, 0.0), (le, 1.0), (gt, 1.0), (neg, 0.0), (ones, 1.0), (m32, 0.0), (own_block, 0.0),
                       (nhalf, -0.5), (state, 0.0)):
            link(g.memset(c[:], val))
        link(select(ident[:], ALU.not_equal, 1.0, 0, -1, 1))
        link(select(le[:], ALU.is_ge, 0.0, 0, 1, -1))
        link(select(gt[:], ALU.is_ge, 0.0, -1, -1, 1))
        link(select(neg[:], ALU.is_ge, MASKED, 0, -1, 1))
        link(g.memset(m32[0:32, 32:64], 1.0))
        link(g.memset(m32[64:96, 96:128], 1.0))
        for b in range(4):
            link(g.memset(own_block[32 * b:32 * b + 32, b:b + 1], 1.0))
        mark(g.memset(conv_in[:, :, 0:3], 0.0), consts)

        def inverse_root(dst, src, width, mean):
            link(g.tensor_scalar(src, src, mean, EPS, ALU.mult, ALU.add))
            return g.tensor_tensor(dst, src, nhalf[:, 0:width], ALU.pow)

        g.wait_ge(ss_ready, NT)
        mark(inverse_root(rs[:, 0:NT], ss[:, 0:NT], NT, 1.0 / D), rs_ready)

        def split(slot, ready, used):
            g.wait_ge(hi_ready, ready)
            g.tensor_tensor(w_lo[:, slot, :], raw[:, slot, :], w_hi[:, slot, :].bitcast(F32),
                            ALU.subtract).then_inc(lo_ready, 1)

        def split_u(u):
            split(u % 4, u + 1, None)

        g.wait_ge(bahi_ready, 1)
        mark(g.tensor_tensor(ba_lo[:], ba_raw[:], ba_hi[:].bitcast(F32), ALU.subtract), balo_ready)
        for u in range(LEAD):
            split_u(u)

        def per_head(ap):
            return ap.unsqueeze(2).to_broadcast([P, H, HD])

        def side_step(name, i):
            f = FILL[name, i]
            t = i
            if name == "sg":
                g.wait_ge(sig_done, i + 1)
                dst = qk_dn[:, i, :] if i < 8 else v_dn[:, i - 8, :]
                mark(g.tensor_tensor(dst, dst, sig[:, i % 2, :], ALU.mult), silu_done)
            elif name == "gk":
                g.wait_ge(g_ready, 1)
                if t >= 2:
                    full(g, FILL["dec", t - 2] + 1)
                mark(g.tensor_tensor(g_mask[:, t % 2], gt[:].unsqueeze(1).to_broadcast([P, H, P]),
                                     g_sb[:, t * H:(t + 1) * H].unsqueeze(2).to_broadcast([P, H, P]), ALU.mult), gmask_ready)
            elif name == "ta":
                g.wait_ge(ssq_ready, t + 1)
                mark(inverse_root(rsq[:, t, :], ssq[:, t, :], 16, 1.0), rsq_ready)
            elif name == "zz":
                g.wait_ge(zsig_done, t + 1)
                link(g.tensor_tensor(z_sb[:, t, :], z_sb[:, t, :],
                                     (u_sb[:] if t % 2 == 0 else w_t[:].rearrange("p a b -> p (a b)")), ALU.mult))
                mark(g.tensor_tensor(heads(z_sb[:, t, :]), heads(z_sb[:, t, :]), dnw[:].unsqueeze(1).to_broadcast([P, H, HD]),
                                     ALU.mult), z_ready)
            elif name == "ex":
                g.wait_ge(blocks_ready, 1)
                if t:
                    freed(g, FILL["uw", t - 1] + 1)
                for dst, src in ((t_bd, t_blocks), (v_bd, v_blocks)):
                    mark(g.tensor_tensor(dst[:].rearrange("p h (b l) -> p h b l", l=B32),
                                         src[:, t * H:(t + 1) * H, :].unsqueeze(2).to_broadcast([P, H, 4, B32]),
                                         own_block[:].unsqueeze(1).unsqueeze(3).to_broadcast([P, H, 4, B32]), ALU.mult), bd_ready)
            elif name == "kk":
                g.wait_ge(be_ready, 1)
                if t:
                    g.wait_ge(sso_ready, t)
                link(g.tensor_tensor(heads(u_sb[:]), heads(k_hat[:, t, :]), per_head(be[:, t * H:(t + 1) * H]), ALU.mult))
                mark(g.tensor_tensor(heads(k_hat[:, t, :]), heads(k_hat[:, t, :]), per_head(eg[:, 32 + t * H:32 + (t + 1) * H]),
                                     ALU.mult), kbg_ready)
            elif name == "on":
                g.wait_ge(o_ready, t + 1)
                mark(g.tensor_tensor(u_sb[:], o_acc[:], o_acc[:], ALU.mult), osq_ready)
            elif name == "oo":
                g.wait_ge(sso_ready, t + 1)
                mark(inverse_root(rso[:], sso[:], H, 1.0 / HD), rso_ready)
            elif name == "op":
                g.wait_ge(on_ready, t + 1)
                mark(g.tensor_tensor(o_acc[:], o_acc[:], z_sb[:, t, :], ALU.mult), y_ready)

        for u in range(U_IN + 1):
            if u < U_IN:
                split_u(u + LEAD)
            for name, i in steps_at(u):
                side_step(name, i)
        for u in range(U_IN, U_OUT):
            split_u(u + LEAD)
            if u - U_IN in (5, 9, 13, 17):
                q = (u - U_IN - 5) // 4
                for m in range(2):
                    g.wait_ge(prod_ready, 4 * q + 2 * m + 2)
                    mark(g.tensor_tensor(m_a[:, m, :], m_a[:, m, :], m_d[:, m, :], ALU.add), m_ready)
                for m in range(2):
                    g.wait_ge(mhi_ready, 2 * q + m + 1)
                    mark(g.tensor_tensor(h_lo[:, 2 * q + m, :], m_a[:, m, :], h_hi[:, 2 * q + m, :].bitcast(F32),
                                         ALU.subtract), mlo_ready)
        for t in range(NT):
            g.wait_ge(ssh_ready, t + 1)
            mark(inverse_root(rs1[:, t:t + 1], ssh[:, t:t + 1], 1, 1.0 / D), rs1_ready)
        for t in range(NT):
            g.wait_ge(ss2_ready, t + 1)
            mark(inverse_root(rs2[:, t:t + 1], ss2[:, t:t + 1], 1, 1.0 / D), rs2_ready)
        n_u = U_ALL - U_OUT - LEAD - 1
        with g.Fori(0, n_u // 4) as i:
            for j in range(4):
                u = U_OUT + LEAD + j
                split(u % 4, i * 4 + (u + 1), None)
        for u in range(U_OUT + LEAD + n_u // 4 * 4, U_ALL):
            split_u(u)
        for t in range(NT):
            g.wait_ge(ssh_ready, NT + t + 1)
            mark(inverse_root(rs1[:, t:t + 1], ssh[:, t:t + 1], 1, 1.0 / D), rsf_ready)

    ctx.close()


NAMES = ["x", "pre_norm_mix", "w_in", "conv_w", "a_log", "dt_bias", "dn_norm", "w_branch_att", "w_branch_dn", "w_out",
         "post_norm_mix", "pre_norm_mlp", "w_mlp_in", "w_mlp_out", "post_norm_mlp"]


def kernel(**inputs):
    import numpy as np
    import concourse.bacc as bacc
    from concourse.bass_utils import run_bass_kernel_spmd

    nc = bacc.Bacc("TRN2", target_bir_lowering=False, num_devices=1)
    arrays, args = {}, []
    for name in NAMES:
        a = np.asarray(inputs[name])
        if name.startswith("pre_norm"):
            a = a[0].reshape(KD, P).T
        elif name == "conv_w":
            a = a[0].reshape(4, 12, P).transpose(2, 1, 0)
        a = np.ascontiguousarray(a)
        arrays["in_" + name] = a
        args.append(nc.dram_tensor("in_" + name, a.shape, mybir.dt.from_np(a.dtype), kind="ExternalInput").ap())
    args.append(nc.dram_tensor("out_0", (1, S, D), F32, kind="ExternalOutput").ap())
    program(nc, *args)
    r = run_bass_kernel_spmd(nc, [arrays], core_ids=[0])
    return r.results[0]["out_0"]
```

```python
from contextlib import ExitStack

import concourse.bass as bass
from concourse import mybir

F32 = mybir.dt.float32
F32R = mybir.dt.float32r
ALU = mybir.AluOpType
ACT = mybir.ActivationFunctionType
AX = mybir.AxisListType

P = 128
D = 1024
S = 512
NT = S // P
KD = D // P
H = 8
HD = 64
W = H * HD
FF = 4 * D
EPS = 1e-6
COL_QK, COL_V, COL_DN, COL_Z, COL_BA, COL_GATE = 0, 2 * W, 3 * W, 6 * W, 7 * W, 7 * W + 2 * H
MASKED = -3.0e38
B32 = 32

RAW = 4
SPL = 4
LEAD = 3
GROUPS = ([(COL_DN + 256 * g, "f") for g in range(6)] + [(COL_QK + 256 * g, "f") for g in range(4)]
          + [(COL_Z, "t"), (COL_V, "t")] + [(COL_GATE + 256 * g, "f") for g in range(8)])


def group_table():
    first, copies, last, out = 0, 0, [0] * 4, []
    turn = 0
    for col, kind in GROUPS:
        if kind == "f":
            banks, n = [turn, turn + 1], 4
            turn = (turn + 2) % 4
        else:
            banks, n = [0, 1, 2, 3], 8
            turn = 0
        need = [last[b] for b in banks]
        for b in banks:
            copies += 1
            last[b] = copies
        out.append((first, banks, copies, need))
        first += n
    return out


TABLE = group_table()
U_IN = 88
U_BR = U_IN + 16
U_OUT = U_BR + 16
U_M1 = U_OUT + 64
U_ALL = U_M1 + 64
UNIT_GROUP = {}
for _g, (_f, _b, _c, _n) in enumerate(TABLE):
    for _u in range(_f, _f + (4 if GROUPS[_g][1] == "f" else 8)):
        UNIT_GROUP[_u] = _g

ROWS = [(1, 6), (6, 11), (11, 14), (14, 17), (17, 19), (19, 21), (21, 22), (22, 24), (24, 25), (25, 27), (27, 28), (28, 29), (29, 30), (30, 31), (31, 32)]


T2_BANK = [2, 3, 4, 5, 2, 3, 4, 5, 6, 7, 2, 3, 4, 5, 6, 7]


def side_steps():
    s = [(4, "ba", 0), (7, "bt", 0), (10, "gm", 0)]
    for m in range(12):
        s += [(4 + 4 * (m // 2) + 2 * (m % 2), "cv", m), (6 + 4 * (m // 2) + 2 * (m % 2), "sg", m)]
    for t in range(NT):
        s += [((12, 15, 17, 20)[t], "gk", t), (21 + 2 * t, "ta", t), ((14, 18, 31, 33)[t], "dec", t), (25 + 2 * t, "ht", t), (26 + 2 * t, "tb", t),
              (29 + 2 * t, "gr", t), (30 + 2 * t, "qt", t), (37 + 2 * t, "tv", t)]
    for g in range(6, len(GROUPS)):
        n = 4 if GROUPS[g][1] == "f" else 8
        s.append((TABLE[g][0] + n, "ev", g))
    s += [(49 + t, "zz", t) for t in range(NT)] + [(49 + 2 * t, "zp", t) for t in range(NT)]
    s += [(37 + j, "bi", j) for j in range(len(ROWS))] + [(37 + len(ROWS), "bo", 0)]
    for t in range(NT):
        b = 55 + 6 * t
        s += [(b if t else b - 1, "ex", t), (b + 2, "lg", t), (b + 3, "lv", t), (b + 3, "lt", t), (b + 4, "l6", t), (b + 5, "l7", t),
              (b + 5, "kk", t), (b + 6, "uw", t), (b + 7, "sa", t), (b + 8, "sb", t), (b + 9, "on", t),
              (b + 10, "oo", t), (b + 11, "op", t), (b + 12, "ot", t)]
    s += [(86, "yp", 0), (87, "yp", 1)]
    for n in range(16):
        s += [(54 + 2 * n, "a1", n), (55 + 2 * n, "an", n), (56 + 2 * n, "a2", n), (58 + 2 * n, "a3", n)]
    rank = {"ev": 0, "an": 1, "ht": 1, "bt": 12, "gm": 12, "uw": 2, "ot": 2, "a3": 3, "a2": 4, "tb": 5, "a1": 20}
    return sorted(s, key=lambda x: (min(x[0], U_IN), x[0] if x[0] > U_IN else 0, rank.get(x[1], 9)))


STEPS = side_steps()
BANKS_OF = {"ba": 1, "bt": 1, "gm": 1, "dec": 2, "ta": 2, "tv": 1, "tb": 2, "gr": 4, "qt": 2, "lg": 2, "lv": 2,
            "lt": 2, "l6": 1, "l7": 1, "uw": 2, "sa": 2, "sb": 2, "ot": 1, "a1": 2, "a2": 2, "a3": 1}


def fills():
    out, f = {}, 2 * KD
    for _, name, i in STEPS:
        out[name, i] = f
        f += BANKS_OF.get(name, 0)
    return out, f


FILL, FILLS = fills()


def steps_at(unit):
    return [(name, i) for u, name, i in STEPS if min(u, U_IN) == unit]


def program(nc, x, pre_norm_mix, w_in, conv_w, a_log, dt_bias, dn_norm, w_branch_att, w_branch_dn, w_out,
            post_norm_mix, pre_norm_mlp, w_mlp_in, w_mlp_out, post_norm_mlp, out):
    ctx = ExitStack()
    base = (nc.sbuf_base + 63) // 64 * 64
    KB = 1024

    def at(name, kb, shape, dt=F32):
        return nc.alloc_sbuf_tensor_at(name, shape, dt, offset=base + int(kb * KB))

    h_hi = at("h_hi", 0, [P, KD, S], F32R)
    h_lo = at("h_lo", 16, [P, KD, S], F32R)
    raw = at("raw", 32, [P, RAW, 512])
    w_hi = at("w_hi", 40, [P, SPL, 512], F32R)
    w_lo = at("w_lo", 48, [P, SPL, 512], F32R)
    x_sb = at("x_sb", 56, [P, NT, D])
    gate_a = at("gate_a", 56, [P, KD, S])
    qk_dn = at("qk_dn", 72, [P, 8, S])
    t_blocks = at("t_blocks", 80, [P, 32, B32])
    v_blocks = at("v_blocks", 84, [P, 32, B32])
    v_dn = at("v_dn", 88, [P, 4, S])
    v_att = at("v_att", 88, [P, NT, W])
    k_hat = at("k_hat", 96, [P, NT, W])
    beta_v = at("beta_v", 104, [P, NT, W])
    neg_l = at("neg_l", 112, [P, 32, P])
    gate_d = at("gate_d", 112, [P, KD, S])
    qk_t = at("qk_t", 128, [P, 32, P])
    xn = at("xn", 128, [P, NT, D])
    z_sb = at("z_sb", 144, [P, NT, W])
    conv_in = at("conv_in", 152, [P, 2, 3 + S])
    decay1 = at("decay1", 144, [P, H, P])
    qk_m = at("qk_m", 148, [P, H, P])
    l_rows = at("l_rows", 152, [P, B32, B32])
    t_rows = at("t_rows", 156, [P, B32, B32])
    t_bd = at("t_bd", 152, [P, H, P])
    v_bd = at("v_bd", 156, [P, H, P])
    sig = at("sig", 160, [P, 2, S])
    g_mask = at("g_mask", 64, [P, 2, H, P])
    decay0 = at("decay0", 164, [P, H, P])
    probs = at("probs", 160, [P, 2, S])
    probs_t = at("probs_t", 164, [P, 2, S])
    junk = at("junk", 168, [P, D])
    q_tok = at("q_tok", 56, [P, NT, W])
    sq_tok = at("sq_tok", 168, [P, 2, W])
    prod = at("prod", 168, [P, B32 * B32])
    gs = at("gs", 168, [P, H, P])
    u_sb = at("u_sb", 172, [P, W])
    w_t = at("w_t", 174, [P, 4, P])
    state = at("state", 176, [P, 4, P])
    qk_att = at("qk_att", 178, [P, 8, S])
    v_new = at("v_new", 194, [P, W])
    o_acc = at("o_acc", 196, [P, W])
    y_hi = at("y_hi", 128, [P, 8, S], F32R)
    y_lo = at("y_lo", 144, [P, 8, S], F32R)
    m_a = at("m_a", 160, [P, 2, S])
    m_d = at("m_d", 164, [P, 2, S])
    x_res = at("x_res", 96, [P, NT, D])
    pn_mix = at("pn_mix", 80, [P, D])
    pn_mlp = at("pn_mlp", 84, [P, D])
    junk2 = at("junk2", 88, [P, D])
    tmp2 = at("tmp2", 168, [P, 2, D])
    hn = at("hn", 56, [P, NT, D])
    act = at("act", 112, [P, FF // P, S])
    a_hi = at("a_hi", 176, [P, 4, S], F32R)
    a_lo = at("a_lo", 184, [P, 4, S], F32R)
    relu = at("relu", 56, [P, 4, S])
    y_out = at("y_out", 56, [P, NT, D])
    off = [198 * KB]

    def small(name, shape, dt=F32):
        n = 4
        for d in shape[1:]:
            n *= d
        t = nc.alloc_sbuf_tensor_at(name, shape, dt, offset=base + off[0])
        off[0] += (n + 31) // 32 * 32
        return t

    ident = small("ident", [P, P])
    le = small("le", [P, P])
    gt = small("gt", [P, P])
    neg = small("neg", [P, P])
    ones = small("ones", [P, P])
    m32 = small("m32", [P, P])
    own_block = small("own_block", [P, 4])
    wpre = small("wpre", [P, KD])
    wmlp = small("wmlp", [P, KD])
    cw = small("cw", [P, 12, 4])
    dnw = small("dnw", [P, HD])
    dtb = small("dtb", [P, H])
    alog = small("alog", [P, H])
    nhalf = small("nhalf", [P, 16])
    ss = small("ss", [P, 16])
    rs = small("rs", [P, 16])
    ba_raw = small("ba_raw", [P, KD, 16])
    ba_w = small("ba_w", [P, KD, 32], F32R)
    ba_tok = small("ba_tok", [P, NT, 16])
    beta = small("beta", [P, 32])
    nbeta = small("nbeta", [P, 32])
    g_sb = small("g_sb", [P, 32])
    eg = small("eg", [P, 96])
    be = small("be", [P, 32])
    sp = small("sp", [P, 6, 32])
    ssq = small("ssq", [P, NT, 16])
    flag = small("flag", [P, 1])
    rsq = small("rsq", [P, NT, 16])
    sso = small("sso", [P, H])
    rso = small("rso", [P, H])
    nmax = small("nmax", [P, 2])
    nmax8 = small("nmax8", [P, 2])
    psumr = small("psumr", [P, 2])
    pinv = small("pinv", [P, 2])
    ssy = small("ssy", [P, 8])
    ssh = small("ssh", [P, NT])
    ss2 = small("ss2", [P, NT])
    rs1 = small("rs1", [P, NT])
    rs2 = small("rs2", [P, NT])
    assert base + off[0] <= nc.sbuf_usable_end if hasattr(nc, "sbuf_usable_end") else True
    ba_t = o_acc
    z_sig = [u_sb[:], w_t[:].rearrange("p a b -> p (a b)"), v_new[:], o_acc[:]]

    bank = [ctx.enter_context(nc.psum_tensor(f"bank{i}", [P, 512], F32)) for i in range(8)]
    side = bank[4:]

    def sem(name):
        return ctx.enter_context(nc.semaphore(name))

    x_in = [sem(f"x_in{t}") for t in range(NT)]
    small_in = sem("small_in")
    ba_in = sem("ba_in")
    raw_in = [sem(f"raw_in{i}") for i in range(RAW)]
    hi_ready = sem("hi_ready")
    lo_ready = sem("lo_ready")
    unit_done = sem("unit_done")
    bank_copied = sem("bank_copied")
    side_full = sem("side_full")
    side_free = [sem(f"side_free{i}") for i in range(4)]
    consts = sem("consts")
    flag_set = sem("flag_set")
    ones_set = sem("ones_set")
    ss_ready = sem("ss_ready")
    rs_ready = sem("rs_ready")
    xn_ready = sem("xn_ready")
    hhi_ready = sem("hhi_ready")
    bahi_ready = sem("bahi_ready")
    balo_ready = sem("balo_ready")
    conv_done = sem("conv_done")
    sig_done = sem("sig_done")
    silu_done = sem("silu_done")
    silu_v_done = sem("silu_v_done")
    ba_args = sem("ba_args")
    ba_acts = sem("ba_acts")
    g_ready = sem("g_ready")
    be_ready = sem("be_ready")
    gmask_ready = sem("gmask_ready")
    ssq_ready = sem("ssq_ready")
    rsq_ready = sem("rsq_ready")
    hat_ready = sem("hat_ready")
    blocks_ready = sem("blocks_ready")
    tbd_ready = sem("tbd_ready")
    vbd_ready = sem("vbd_ready")
    kbg_ready = sem("kbg_ready")
    o_ready = sem("o_ready")
    osq_ready = sem("osq_ready")
    sso_ready = sem("sso_ready")
    rso_ready = sem("rso_ready")
    on_ready = sem("on_ready")
    y_ready = sem("y_ready")
    zsig_done = sem("zsig_done")
    z_ready = sem("z_ready")
    max_ready = sem("max_ready")
    p_ready = sem("p_ready")
    yhi_ready = sem("yhi_ready")
    ylo_ready = sem("ylo_ready")
    gates_ready = sem("gates_ready")
    prod_ready = sem("prod_ready")
    m_ready = sem("m_ready")
    mhi_ready = sem("mhi_ready")
    mlo_ready = sem("mlo_ready")
    xr_in = sem("xr_in")
    pn_in = sem("pn_in")
    ssy_ready = sem("ssy_ready")
    rs1_ready = sem("rs1_ready")
    x2_ready = sem("x2_ready")
    x2_pool = sem("x2_pool")
    y_done = sem("y_done")
    y_scaled = sem("y_scaled")
    ss2_ready = sem("ss2_ready")
    rs2_ready = sem("rs2_ready")
    hn_ready = sem("hn_ready")
    t2_full = sem("t2_full")
    t2_hi = sem("t2_hi")
    t2_lo = sem("t2_lo")
    relu_done = sem("relu_done")
    act_ready = sem("act_ready")
    ahi_ready = sem("ahi_ready")
    alo_ready = sem("alo_ready")
    y_pool = sem("y_pool")
    rsf_ready = sem("rsf_ready")
    y_final = sem("y_final")
    stored = sem("stored")
    act_chain = sem("act_chain")
    dve_chain = sem("dve_chain")
    pool_chain = sem("pool_chain")

    w1 = w_in[0]
    xt = x[0].rearrange("(t p) d -> t p d", p=P)
    ot = out[0].rearrange("(t p) d -> t p d", p=P)

    def unit_source(u):
        if u < U_IN:
            g = UNIT_GROUP[u]
            col, kind = GROUPS[g]
            j = u - TABLE[g][0]
            if kind == "f":
                return w1[j * 256:(j + 1) * 256, col:col + 256].rearrange("(k p) c -> p k c", p=P)
            return w1[j * P:(j + 1) * P, col:col + 512]
        if u < U_BR:
            j = u - U_IN
            w = (w_branch_dn, w_branch_att)[j // 2 % 2][0]
            return w[j % 2 * 256:j % 2 * 256 + 256, j // 4 * 256:j // 4 * 256 + 256].rearrange("(k p) c -> p k c", p=P)
        j = u - U_BR
        return w_out[0][j // 2 * P:j // 2 * P + P, j % 2 * 512:j % 2 * 512 + 512]

    def full(eng, f):
        eng.wait_ge(side_full, f + 1)

    def freed(eng, f):
        if f >= 0:
            eng.wait_ge(side_free[f % 4], f // 4 + 1)

    def heads(ap):
        return ap.rearrange("p (h d) -> p h d", d=HD)

    def block_diag(eng, dst, src, t):
        return eng.tensor_tensor(dst[:].rearrange("p h (b l) -> p h b l", l=B32),
                                 src[:, t * H:(t + 1) * H, :].unsqueeze(2).to_broadcast([P, H, 4, B32]),
                                 own_block[:].unsqueeze(1).unsqueeze(3).to_broadcast([P, H, 4, B32]), ALU.mult)

    block = ctx.enter_context(nc.Block())

    @block.sync
    def _(sp_):
        def load(u, slot, source, used):
            if used is not None:
                sp_.wait_ge(lo_ready, used)
            dst = raw[:, slot, :]
            if len(source.shape) == 3:
                dst = dst.rearrange("p (k c) -> p k c", k=2)
            sp_.dma_start(dst, source).then_inc(raw_in[slot], 16)

        for t in range(NT):
            sp_.dma_start(x_sb[:, t, :], xt[t]).then_inc(x_in[t], 16)
            if t in (1, 2):
                load(t - 1, t - 1, unit_source(t - 1), None)
            if t == 1:
                sp_.dma_start(wpre[:], pre_norm_mix).then_inc(small_in, 16)
        for u in range(2, U_OUT):
            if u == 4:
                for dst, src in ((wmlp, pre_norm_mlp), (cw, conv_w),
                                 (dnw, dn_norm[0].partition_broadcast(P)), (dtb, dt_bias[0].partition_broadcast(P)),
                                 (alog, a_log[0].partition_broadcast(P))):
                    sp_.dma_start(dst[:], src).then_inc(small_in, 16)
                sp_.dma_start(ba_raw[:], w1[:, COL_BA:COL_BA + 16].rearrange("(k p) c -> p k c", p=P)).then_inc(ba_in, 16)
            load(u, u % RAW, unit_source(u), u - RAW + 1 if u >= RAW else None)
            if u == U_IN + 8:
                sp_.wait_ge(ylo_ready, 4)
                sp_.dma_start(x_res[:], x[0].rearrange("(t p) d -> p t d", p=P)).then_inc(xr_in, 16)
                sp_.dma_start(pn_mix[:], post_norm_mix[0].partition_broadcast(P)).then_inc(pn_in, 16)
                sp_.dma_start(pn_mlp[:], post_norm_mlp[0].partition_broadcast(P)).then_inc(pn_in, 16)
        with sp_.Fori(0, 16) as g:
            for j in range(4):
                load(0, j, w_mlp_in[0][j * 256:(j + 1) * 256, bass.ds(g * 256, 256)].rearrange("(k p) c -> p k c", p=P),
                     g * 4 + (U_OUT + j - RAW + 1))
        with sp_.Fori(0, 16) as k2:
            for j in range(4):
                load(0, j, w_mlp_out[0][bass.ds(k2 * 256 + j // 2 * P, P), j % 2 * 512:j % 2 * 512 + 512],
                     k2 * 4 + (U_M1 + j - RAW + 1))
        for t in range(NT):
            sp_.wait_ge(y_final, t + 1)
            sp_.dma_start(ot[t][:, 0:512], y_out[:, t, 0:512]).then_inc(stored, 16)
            sp_.wait_ge(y_pool, t + 1)
            sp_.dma_start(ot[t][:, 512:], y_out[:, t, 512:]).then_inc(stored, 16)
        sp_.wait_ge(stored, 2 * 16 * NT)

    @block.tensor
    def _(pe):
        def three(o, s_hi, s_lo, m_hi, m_lo, start, stop):
            pe.matmul(o, s_hi, m_hi, start=start, stop=False, skip_group_check=True)
            pe.matmul(o, s_hi, m_lo, start=False, stop=False, skip_group_check=True)
            return pe.matmul(o, s_lo, m_hi, start=False, stop=stop, skip_group_check=True)

        def open_fill(f):
            if f >= 4:
                pe.wait_ge(side_free[f % 4], f // 4)
            return side[f % 4]

        def x_transposes(half, ks):
            pe.wait_ge(xn_ready, 2 * half + 2)
            for k in ks:
                b = open_fill(half * KD + k)
                for t in range(2):
                    i = pe.transpose(b[:, t * P:(t + 1) * P], xn[:, 2 * half + t, k * P:(k + 1) * P], ident[:])
                i.then_inc(side_full, 1)

        def unit(u, toks=slice(0, S), done=True):
            s = u % SPL
            pe.wait_ge(lo_ready, u + 1)
            if u < U_IN:
                g = UNIT_GROUP[u]
                first, banks, _, need = TABLE[g]
                j = u - first
                if GROUPS[g][1] == "f":
                    for kk in range(2):
                        k = 2 * j + kk
                        for m in range(2):
                            if k == 0 and need[m]:
                                pe.wait_ge(bank_copied, need[m])
                            c = slice(kk * 256 + m * P, kk * 256 + m * P + P)
                            i = three(bank[banks[m]][:, toks], w_hi[:, s, c], w_lo[:, s, c], h_hi[:, k, toks],
                                      h_lo[:, k, toks], k == 0, k == KD - 1)
                else:
                    for t in range(NT):
                        if j == 0 and need[t]:
                            pe.wait_ge(bank_copied, need[t])
                        c = slice(t * P, t * P + P)
                        i = three(bank[t][:], h_hi[:, j, c], h_lo[:, j, c], w_hi[:, s, :], w_lo[:, s, :],
                                  j == 0, j == KD - 1)
            elif u < U_BR:
                g, b, j = (u - U_IN) // 4, (u - U_IN) // 2 % 2, u % 2
                if j == 0 and b == 0:
                    if g == 0:
                        pe.wait_ge(bank_copied, TABLE[-1][2])
                    if g == 1:
                        for f in range(FILLS - 4, FILLS):
                            freed(pe, f)
                    if g >= 2:
                        pe.wait_ge(prod_ready, 4 * (g - 1))
                if g == 0:
                    pe.wait_ge(ylo_ready, 2 * b + j + 1)
                for kk in range(2):
                    k = 2 * j + kk
                    for m in range(2):
                        c = slice(kk * 256 + m * P, kk * 256 + m * P + P)
                        i = three(bank[g % 2 * 4 + b * 2 + m][:], w_hi[:, s, c], w_lo[:, s, c],
                                  y_hi[:, b * 4 + k, :], y_lo[:, b * 4 + k, :], k == 0, k == 3)
            else:
                pe.wait_ge(mlo_ready, (u - U_BR) // 2 + 1)
                for t in range(NT):
                    i = out_part(u, t)
            if done:
                i.then_inc(unit_done, 1)

        def out_part(u, t):
            k, half, s = (u - U_BR) // 2, u % 2, u % SPL
            c = slice(t * P, t * P + P)
            return three(bank[2 * t + half][:], h_hi[:, k, c], h_lo[:, k, c], w_hi[:, s, :], w_lo[:, s, :],
                         k == 0, k == KD - 1)

        def side_step(name, i):
            f = FILL[name, i]
            t = i
            tok = slice(t * P, (t + 1) * P) if t < NT else None
            if name == "ba":
                pe.wait_ge(balo_ready, 1)
                b = open_fill(f)
                for k in range(KD):
                    pe.matmul(b[0:32, :], ba_w[:, k, :], h_hi[:, k, :], start=k == 0, stop=False, skip_group_check=True)
                    x_ = pe.matmul(b[0:16, :], ba_w[:, k, 0:16], h_lo[:, k, :], start=False, stop=k == KD - 1,
                                   skip_group_check=True)
                x_.then_inc(side_full, 1)
            elif name == "bt":
                freed(pe, FILL["ba", 0])
                b = open_fill(f)
                for t in range(NT):
                    x_ = pe.transpose(b[:, 32 * t:32 * t + 32], ba_t[0:32, t * P:(t + 1) * P], ident[0:32, 0:32])
                x_.then_inc(side_full, 1)
            elif name == "gm":
                pe.wait_ge(g_ready, 1)
                b = open_fill(f)
                pe.matmul(b[:, 0:32], le[:], g_sb[:], start=True, stop=True)
                pe.matmul(b[:, 32:64], gt[:], g_sb[:], start=True, stop=True)
                pe.matmul(b[:, 64:96], ones[:], g_sb[:], start=True, stop=True).then_inc(side_full, 1)
            elif name == "dec":
                pe.wait_ge(gmask_ready, t + 1)
                for q in range(2):
                    pe.matmul(open_fill(f + q)[:], le[:], g_mask[:, t % 2, 4 * q:4 * q + 4, :], start=True,
                              stop=True).then_inc(side_full, 1)
            elif name in ("ta", "tv"):
                for q, (src, m0) in enumerate(((qk_dn, 0), (qk_dn, 4)) if name == "ta" else ((v_dn, 0),)):
                    pe.wait_ge(*((silu_done, 8) if name == "ta" else (silu_v_done, 4)))
                    b = open_fill(f + q)
                    for m in range(4):
                        x_ = pe.transpose(b[:, m * P:(m + 1) * P], src[:, m0 + m, tok], ident[:])
                    x_.then_inc(side_full, 1)
            elif name == "tb":
                for q, src in enumerate((k_hat[:, t, :], q_tok[:, t, :])):
                    pe.wait_ge(hat_ready, 2 * t + 1 + q)
                    b = open_fill(f + q)
                    for m in range(4):
                        x_ = pe.transpose(b[:, m * P:(m + 1) * P], src[:, m * P:(m + 1) * P], ident[:])
                    x_.then_inc(side_full, 1)
            elif name == "gr":
                freed(pe, FILL["tb", t])
                freed(pe, FILL["tb", t] + 1)
                for q in range(4):
                    r = slice(q % 2 * HD, q % 2 * HD + HD)
                    b = open_fill(f + q)
                    for pair in range(4):
                        x_ = pe.matmul(b[:, pair * P:(pair + 1) * P], qk_dn[r, (0 if q >= 2 else 4) + pair, tok],
                                       qk_dn[r, 4 + pair, tok], start=True, stop=True)
                    x_.then_inc(side_full, 1)
            elif name == "qt":
                freed(pe, FILL["gr", t] + 3)
                for q in range(2):
                    b = open_fill(f + q)
                    for h in range(4):
                        x_ = pe.transpose(b[:, h * P:(h + 1) * P], qk_m[:, 4 * q + h, :], ident[:])
                    x_.then_inc(side_full, 1)
            elif name in ("lg", "lv", "lt"):
                if name == "lg":
                    pe.wait_ge(vbd_ready, t + 1)
                elif name == "lv":
                    pe.wait_ge(tbd_ready, t + 1)
                    freed(pe, FILL["lg", t])
                    freed(pe, FILL["lg", t] + 1)
                for q in range(2):
                    b = open_fill(f + q)
                    for h in range(4 * q, 4 * q + 4):
                        lhs, rhs = {"lg": (neg_l[:, 8 * t + h, :], v_bd[:, h, :]), "lv": (t_bd[:, h, :], gs[:, h, :]),
                                    "lt": (gs[:, h, :], t_bd[:, h, :])}[name]
                        x_ = pe.matmul(b[:, h % 4 * P:h % 4 * P + P], lhs, rhs, start=True, stop=True)
                    x_.then_inc(side_full, 1)
            elif name == "l6":
                for q in range(2):
                    freed(pe, FILL["lv", t] + q)
                    freed(pe, FILL["lt", t] + q)
                b = open_fill(f)
                for h in range(H):
                    x_ = pe.matmul(b[0:64, h * 64:h * 64 + 64], neg_l[64:128, 8 * t + h, 0:64], v_bd[64:128, h, 64:128],
                                   start=True, stop=True)
                x_.then_inc(side_full, 1)
            elif name == "l7":
                freed(pe, FILL["l6", t])
                b = open_fill(f)
                for h in range(H):
                    x_ = pe.matmul(b[0:64, h * 64:h * 64 + 64], t_bd[0:64, h, 0:64],
                                   gs[0:64, h // 2, h % 2 * 64:h % 2 * 64 + 64], start=True, stop=True)
                x_.then_inc(side_full, 1)
            elif name == "uw":
                freed(pe, FILL["l7", t])
                pe.wait_ge(kbg_ready, t + 1)
                b = open_fill(f)
                for h in range(H):
                    r = slice(h % 2 * HD, h % 2 * HD + HD)
                    x_ = pe.matmul(b[r, h // 2 * P:h // 2 * P + P], u_sb[:, h * HD:(h + 1) * HD], v_bd[:, h, :],
                                   start=True, stop=True)
                x_.then_inc(side_full, 1)
                b = open_fill(f + 1)
                for h in range(H):
                    x_ = pe.matmul(b[:, h * HD:(h + 1) * HD], v_bd[:, h, :], beta_v[:, t, h * HD:(h + 1) * HD],
                                   start=True, stop=True)
                x_.then_inc(side_full, 1)
            elif name == "sa":
                freed(pe, FILL["uw", t])
                if t:
                    freed(pe, FILL["sb", t - 1] + 1)
                for q in range(2):
                    b = open_fill(f + q)
                    for pair in range(4):
                        x_ = pe.matmul(b[:, pair * P:(pair + 1) * P], w_t[:, pair, :] if q == 0 else qk_dn[:, pair, tok],
                                       state[:, pair, :], start=True, stop=True)
                    x_.then_inc(side_full, 1)
            elif name == "sb":
                freed(pe, FILL["sa", t])
                pe.wait_ge(kbg_ready, t + 1)
                freed(pe, FILL["qt", t] + 1)
                b = open_fill(f)
                for h in range(H):
                    hc = slice(h * HD, (h + 1) * HD)
                    x_ = pe.matmul(b[:, hc], qk_t[:, 8 * t + h, :], v_new[:, hc], start=True, stop=True)
                x_.then_inc(side_full, 1)
                b = open_fill(f + 1)
                for h in range(H):
                    hc = slice(h * HD, (h + 1) * HD)
                    r = slice(h % 2 * HD, h % 2 * HD + HD)
                    x_ = pe.matmul(b[r, h // 2 * HD:h // 2 * HD + HD], k_hat[:, t, hc], v_new[:, hc], start=True, stop=True)
                x_.then_inc(side_full, 1)
            elif name == "ot":
                pe.wait_ge(y_ready, t + 1)
                b = open_fill(f)
                for m in range(4):
                    x_ = pe.transpose(b[:, m * P:(m + 1) * P], o_acc[:, m * P:(m + 1) * P], ident[:])
                x_.then_inc(side_full, 1)
            elif name == "a1":
                t, pair = i // 4, i % 4
                pe.wait_ge(bank_copied, TABLE[9][2])
                for hh in range(2):
                    r = slice(hh * HD, hh * HD + HD)
                    pe.matmul(open_fill(f + hh)[:, 0:(t + 1) * P], qk_att[r, pair, t * P:(t + 1) * P],
                              qk_att[r, 4 + pair, 0:(t + 1) * P], start=True, stop=True).then_inc(side_full, 1)
            elif name == "a2":
                t = i // 4
                for hh in range(2):
                    pe.wait_ge(p_ready, 2 * i + 1 + hh)
                    b = open_fill(f + hh)
                    for kt in range(t + 1):
                        x_ = pe.transpose(b[:, kt * P:(kt + 1) * P], probs[:, hh, kt * P:(kt + 1) * P], ident[:])
                    x_.then_inc(side_full, 1)
            elif name == "a3":
                t, pair = i // 4, i % 4
                pe.wait_ge(bank_copied, TABLE[11][2])
                freed(pe, FILL["a2", i])
                freed(pe, FILL["a2", i] + 1)
                b = open_fill(f)
                for hh in range(2):
                    h = 2 * pair + hh
                    for kt in range(t + 1):
                        x_ = pe.matmul(b[hh * HD:hh * HD + HD, 0:P], v_att[:, kt, h * HD:(h + 1) * HD],
                                       probs_t[:, hh, kt * P:(kt + 1) * P], start=kt == 0, stop=kt == t)
                x_.then_inc(side_full, 1)

        def keep_warm(n):
            for _ in range(n):
                pe.matmul(bank[0][:, 0:P], ones[:], ones[:], start=True, stop=True)

        pe.wait_ge(ones_set, 1)
        keep_warm(22)
        pe.wait_ge(consts, 1)
        x_transposes(0, range(KD))
        for u in range(4):
            freed(pe, 2 * u)
            freed(pe, 2 * u + 1)
            unit(u, slice(0, 256), False)
            if u == 1:
                x_transposes(1, range(0, 4))
            if u >= 2:
                x_transposes(1, range(2 * u, 2 * u + 2))
        for u in range(4):
            freed(pe, KD + 2 * u)
            freed(pe, KD + 2 * u + 1)
            unit(u, slice(256, 512))
        for u in range(4, U_IN):
            unit(u)
            for name, i in steps_at(u):
                side_step(name, i)
        for name, i in steps_at(U_IN):
            side_step(name, i)
        for u in range(U_IN, U_BR):
            unit(u)
        pe.wait_ge(lo_ready, U_BR + 2)
        pe.wait_ge(mlo_ready, 1)
        for tt in (0, 2):
            for u in (U_BR, U_BR + 1):
                pe.wait_ge(prod_ready, 12 if tt == 0 else 14 if u == U_BR else 16)
                out_part(u, tt)
                i = out_part(u, tt + 1)
                if tt == 2:
                    i.then_inc(unit_done, 1)
        for u in range(U_BR + 2, U_OUT - 4):
            unit(u)
        pe.wait_ge(mlo_ready, KD)
        for t in range(NT):
            for half in range(2):
                if t == 0:
                    pe.wait_ge(lo_ready, U_OUT - 1 + half)
                i = out_part(U_OUT - 4 + half, t)
                if t == NT - 1:
                    i.then_inc(unit_done, 1)
                i = out_part(U_OUT - 2 + half, t)
                if t == NT - 1 and half == 1:
                    i.then_inc(unit_done, 2)
                else:
                    i.then_inc(y_done, 1)

        def h_transposes(fs):
            for f in fs:
                half, k = f // KD, f % KD
                pe.wait_ge(hn_ready, 2 * half + 2)
                before = [g for g in range(f) if T2_BANK[g] == T2_BANK[f]]
                if before:
                    pe.wait_ge(t2_lo, before[-1] + 1)
                for t in range(2):
                    i = pe.transpose(bank[T2_BANK[f]][:, t * P:t * P + P], hn[:, 2 * half + t, k * P:(k + 1) * P], ident[:])
                i.then_inc(t2_full, 1)

        def mlp_in_unit(s, b, toks):
            for kk in range(2):
                for m in range(2):
                    c = slice(kk * 256 + m * P, kk * 256 + m * P + P)
                    k = 2 * s + kk
                    x_ = three(bank[b + m][:, toks], w_hi[:, s, c], w_lo[:, s, c], h_hi[:, k, toks], h_lo[:, k, toks],
                               k == 0, k == KD - 1)
            return x_

        pe.wait_ge(hn_ready, 1)
        keep_warm(8)
        h_transposes(range(0, 4))
        for j in range(4):
            pe.wait_ge(t2_lo, 2 * j + 2)
            pe.wait_ge(lo_ready, U_OUT + j + 1)
            mlp_in_unit(j, 0, slice(0, 256))
            if j < 2:
                h_transposes(range(4 + 2 * j, 6 + 2 * j))
        h_transposes(range(KD, 2 * KD))
        for j in range(4):
            pe.wait_ge(t2_lo, KD + 2 * j + 2)
            mlp_in_unit(j, 0, slice(256, 512)).then_inc(unit_done, 1)

        def mlp_in(i, first):
            for q in range(1 if first else 0, 2):
                if not first:
                    pe.wait_ge(relu_done, i * 4 + (2 * q - 2))
                for j in range(4):
                    pe.wait_ge(lo_ready, i * 8 + (U_OUT + 4 * q + j + 1))
                    mlp_in_unit(j, 2 * q, slice(0, S)).then_inc(unit_done, 1)

        mlp_in(0, True)
        with pe.Fori(1, 8) as i:
            mlp_in(i, False)

        def mlp_out_part(j, t, start, stop):
            c = slice(t * P, t * P + P)
            return three(bank[2 * t + j % 2][:], a_hi[:, j // 2, c], a_lo[:, j // 2, c], w_hi[:, j % 4, :],
                         w_lo[:, j % 4, :], start, stop)

        def mlp_out(i, first, last):
            for j in range(4 if last else 8):
                if j % 2 == 0:
                    pe.wait_ge(alo_ready, i * 4 + (j // 2 + 1))
                pe.wait_ge(lo_ready, i * 8 + (U_M1 + j + 1))
                for t in (2, 3, 0, 1):
                    if first and j == 0 and t < 2:
                        pe.wait_ge(relu_done, 30 + 2 * t)
                    x_ = mlp_out_part(j, t, first and j < 2, False)
                x_.then_inc(unit_done, 1)

        mlp_out(0, True, False)
        with pe.Fori(1, 7) as i:
            mlp_out(i, False, False)
        mlp_out(7, False, True)
        for t in range(NT):
            for half in range(2):
                if t == 0:
                    pe.wait_ge(lo_ready, U_ALL - 3 + half)
                    pe.wait_ge(alo_ready, 31)
                mlp_out_part(4 + half, t, False, False)
                if t == 0:
                    pe.wait_ge(lo_ready, U_ALL - 1 + half)
                    pe.wait_ge(alo_ready, 32)
                mlp_out_part(6 + half, t, False, True).then_inc(y_done, 1)

    @block.scalar
    def _(a):
        n = {}

        def mark(i, s):
            n[s.name] = n.get(s.name, 0) + 1
            i.then_inc(s, 1)
            a.wait_ge(s, n[s.name])

        def link(i):
            mark(i, act_chain)

        def release(i, f):
            i.then_inc(side_free[f % 4], 1)
            a.wait_ge(side_free[f % 4], f // 4 + 1)

        def copy(o, i_, scale=1.0):
            return a.activation(o, i_, ACT.Copy, scale=scale)

        a.wait_ge(flag_set, 1)
        link(a.activation(flag[:], flag[:], ACT.Square))

        def square(t):
            a.wait_ge(x_in[t], 16)
            mark(a.activation(junk[:], x_sb[:, t, :], ACT.Square, accum_out=ss[:, t:t + 1]), ss_ready)

        def h_part(half, ks=range(KD)):
            for k in ks:
                full(a, half * KD + k)
                mark(copy(h_hi[:, k, 256 * half:256 * half + 256], side[k % 4][:, 0:256], wpre[:, k:k + 1]), hhi_ready)

        def split(u, slot, loaded, used):
            a.wait_ge(raw_in[slot], loaded)
            if used is not None:
                a.wait_ge(unit_done, used)
            copy(w_hi[:, slot, :], raw[:, slot, :]).then_inc(hi_ready, 1)

        def split_u(u):
            split(u, u % 4, 16 * (u // 4 + 1), u - 3 if u >= 4 else None)

        square(0)
        square(1)
        split_u(0)
        square(2)
        split_u(1)
        a.wait_ge(small_in, 16)
        h_part(0, range(0, 4))
        square(3)
        h_part(0, range(4, 8))
        split_u(2)
        split_u(3)
        h_part(1)
        a.wait_ge(ba_in, 16)
        mark(copy(ba_w[:, :, 0:16], ba_raw[:]), bahi_ready)

        def side_step(name, i):
            f = FILL[name, i]
            t = i
            tok = slice(t * P, (t + 1) * P) if t < NT else None
            if name == "yp":
                if i == 0:
                    a.wait_ge(y_ready, NT)
                y_hi_part(i)
            if name == "ba":
                full(a, f)
                release(copy(ba_t[0:32, :], side[f % 4][0:32, :]), f)
            elif name == "bt":
                a.wait_ge(ba_args, 2)
                mark(a.activation(beta[:].rearrange("p (t h) -> p t h", h=H), ba_tok[:, :, 0:H], ACT.Sigmoid), ba_acts)
                mark(a.activation(sp[:, 2, :], sp[:, 1, :], ACT.Exp), ba_acts)
                mark(a.activation(alog[:], alog[:], ACT.Exp), ba_acts)
            elif name == "gm":
                full(a, f)
                release(a.activation(eg[:], side[f % 4][:, 0:96], ACT.Exp), f)
            elif name == "cv":
                first, banks, copies, _ = TABLE[i // 2]
                a.wait_ge(unit_done, first + 4)
                if i >= 2:
                    a.wait_ge(conv_done, i - 1)
                else:
                    a.wait_ge(consts, 1)
                mark(copy(conv_in[:, i % 2, 3:3 + S], bank[banks[i % 2]][:]), bank_copied)
            elif name == "sg":
                a.wait_ge(conv_done, i + 1)
                if 2 <= i < 10:
                    a.wait_ge(silu_done, i - 1)
                elif i >= 10:
                    a.wait_ge(silu_v_done, i - 9)
                src = qk_dn[:, i, :] if i < 8 else v_dn[:, i - 8, :]
                mark(a.activation(sig[:, i % 2, :], src, ACT.Sigmoid), sig_done)
            elif name == "ev":
                first, banks, copies, _ = TABLE[i]
                a.wait_ge(unit_done, first + (4 if GROUPS[i][1] == "f" else 8))
                if i >= 16:
                    full(a, FILL["l6", i - 16])
                for m, b in enumerate(banks):
                    if i < 10:
                        dst = qk_att[:, 2 * (i - 6) + m, :]
                    elif i == 10:
                        dst = z_sb[:, m, :]
                    elif i == 11:
                        dst = v_att[:, m, :]
                    elif i < 16:
                        dst = gate_a[:, 2 * (i - 12) + m, :]
                    else:
                        dst = gate_d[:, 2 * (i - 16) + m, :]
                    mark(copy(dst, bank[b][:]), bank_copied)
            elif name == "dec":
                if t >= 2:
                    freed(a, FILL["gr", t - 2] + 3)
                d = (decay0, decay1)[t % 2]
                for q in range(2):
                    full(a, f + q)
                    release(a.activation(d[:, 4 * q:4 * q + 4, :], side[(f + q) % 4][:].rearrange("p (h j) -> p h j", j=P),
                                         ACT.Exp), f + q)
            elif name == "ta":
                full(a, f)
                if t:
                    a.wait_ge(ssq_ready, t)
                link(a.activation(sq_tok[:, 0, :], side[f % 4][:], ACT.Square))
                release(copy(q_tok[:, t, :], side[f % 4][:]), f)
                full(a, f + 1)
                link(a.activation(sq_tok[:, 1, :], side[(f + 1) % 4][:], ACT.Square))
                release(copy(k_hat[:, t, :], side[(f + 1) % 4][:]), f + 1)
            elif name == "tb":
                full(a, f + 1)
                release(copy(qk_dn[:, 0:4, tok], side[(f + 1) % 4][:].rearrange("p (m t) -> p m t", t=P), HD ** -0.5), f + 1)
            elif name == "zz":
                mark(a.activation(z_sig[t], z_sb[:, t, :], ACT.Sigmoid), zsig_done)
            elif name == "l6":
                full(a, f)
                release(copy(gs[0:64, 0:4, :], side[f % 4][0:64, :].rearrange("p (h j) -> p h j", j=P)), f)
            elif name == "l7":
                full(a, f)
                release(copy(v_bd[0:64, :, 64:128], side[f % 4][0:64, :].rearrange("p (h j) -> p h j", j=64)), f)
            elif name == "uw":
                full(a, f)
                release(copy(w_t[:], side[f % 4][:].rearrange("p (h j) -> p h j", j=P)), f)
                full(a, f + 1)
                release(copy(u_sb[:], side[(f + 1) % 4][:]), f + 1)
            elif name == "ot":
                full(a, f)
                release(copy(qk_dn[:, 0:4, tok], side[f % 4][:].rearrange("p (m t) -> p m t", t=P)), f)
            elif name == "a1":
                t = i // 4
                for hh in range(2):
                    a.wait_ge(max_ready, 2 * i + 1 + hh)
                    if i and hh == 0:
                        full(a, FILL["a2", i - 1] + 1)
                    release(a.activation(probs[:, hh, 0:(t + 1) * P], side[(f + hh) % 4][:, 0:(t + 1) * P], ACT.Exp,
                                         bias=nmax8[:, hh:hh + 1], scale=HD ** -0.5, accum_out=psumr[:, hh:hh + 1]), f + hh)
            elif name == "a2":
                t = i // 4
                full(a, f)
                if i:
                    full(a, FILL["a3", i - 1])
                release(copy(probs_t[:, 0, 0:(t + 1) * P], side[f % 4][:, 0:(t + 1) * P]), f)

        def y_hi_part(j):
            src = (qk_dn, qk_att)[j // 2]
            mark(copy(y_hi[:, 2 * j:2 * j + 2, :], src[:, 2 * (j % 2):2 * (j % 2) + 2, :]), yhi_ready)

        for u in range(1, U_IN + 1):
            steps = steps_at(u)
            if steps and steps[0][0] == "ev":
                side_step(*steps.pop(0))
            if u < U_IN:
                split_u(u + LEAD)
            for name, i in steps:
                side_step(name, i)

        for f in range(FILLS - 4, FILLS):
            freed(a, f)
        y_hi_part(2)
        y_hi_part(3)
        for u in range(U_IN, U_OUT - LEAD):
            split_u(u + LEAD)
            if u < U_BR and (u - U_IN) % 4 == 0:
                g = (u - U_IN) // 4
                for gt_ in (gate_a, gate_d):
                    mark(a.activation(gt_[:, 2 * g:2 * g + 2, :], gt_[:, 2 * g:2 * g + 2, :], ACT.Sigmoid), gates_ready)
            if u - U_IN in (5, 9, 13, 17):
                g = (u - U_IN - 5) // 4
                for m in range(2):
                    a.wait_ge(m_ready, 2 * g + m + 1)
                    mark(copy(h_hi[:, 2 * g + m, :], m_a[:, m, :]), mhi_ready)

        def square_y(t, done0):
            for half in range(2):
                b = 2 * t + half
                if done0 == 0 and b == 7:
                    a.wait_ge(unit_done, U_OUT)
                else:
                    a.wait_ge(y_done, done0 + b + 1)
                mark(a.activation(junk2[:, 0:512], bank[b][:], ACT.Square, accum_out=ssy[:, b:b + 1]), ssy_ready)

        def square_x2(t):
            a.wait_ge(x2_ready, t + 1 if t < 2 else 2 * t)
            if t < 2:
                a.wait_ge(x2_pool, t + 1)
            mark(a.activation(junk2[:], x_res[:, t, :], ACT.Square, accum_out=ss2[:, t:t + 1]), ss2_ready)

        def h2_part(fs):
            for f in fs:
                half, k = f // KD, f % KD
                a.wait_ge(t2_full, f + 1)
                mark(copy(h_hi[:, k, 256 * half:256 * half + 256], bank[T2_BANK[f]][:, 0:256], wmlp[:, k:k + 1]), t2_hi)

        square_y(0, 0)
        square_y(1, 0)
        square_x2(0)
        square_y(2, 0)
        square_x2(1)
        split_u(U_OUT)
        square_y(3, 0)
        split_u(U_OUT + 1)
        split_u(U_OUT + 2)
        h2_part(range(0, 4))
        split_u(U_OUT + 3)
        square_x2(2)
        h2_part((4, 5))
        h2_part((6, 7))
        square_x2(3)
        h2_part(range(8, 16))

        def relu_group(i, q, first):
            a.wait_ge(unit_done, i * 8 + (U_OUT + 4 * q + 4))
            for m in range(2):
                if not first:
                    a.wait_ge(act_ready, i * 4 + (2 * q + m + 1 - 4))
                a.activation(relu[:, 2 * q + m, :], bank[2 * q + m][:], ACT.Relu).then_inc(relu_done, 1)

        def mlp_in(i, first, last=False):
            for j in range(8):
                u = U_OUT + LEAD + j
                if not (first and j == 0):
                    split(None, u % 4, i * 32 + 16 * (u // 4 + 1), i * 8 + (u - 3))
                if last and j == 5:
                    act_hi(0, 0, False)
                    act_hi(0, 1, False)
                if j in (3, 7):
                    relu_group(i, j // 4, first)

        def act_hi(i, kt, used):
            a.wait_ge(act_ready, i * 4 + (kt + 1) if not isinstance(i, int) else 4 * i + kt + 1)
            if used:
                a.wait_ge(unit_done, i * 8 + (U_M1 + 2 * (kt - 4) + 2))
            copy(a_hi[:, kt % 4, :], act[:, bass.ds(i * 4 + kt, 1), :].rearrange("p a s -> p (a s)")).then_inc(ahi_ready, 1)

        mlp_in(0, True)
        with a.Fori(1, 7) as i:
            mlp_in(i, False)
        mlp_in(7, False, True)

        def mlp_out(i, first, last):
            for j in range(8):
                u = U_M1 + LEAD + j
                if not (last and j >= 8 - LEAD):
                    split(None, u % 4, i * 32 + 16 * (u // 4 + 1), i * 8 + (u - 3))
                if j % 2 == 0 and not (last and j >= 4):
                    act_hi(i, j // 2 + 2, not (first and j < 4))

        mlp_out(0, True, False)
        with a.Fori(1, 7) as i:
            mlp_out(i, False, False)
        mlp_out(7, False, True)
        for t in range(NT):
            square_y(t, 7)

    @block.vector
    def _(v):
        n = {}

        def mark(i, s):
            n[s.name] = n.get(s.name, 0) + 1
            i.then_inc(s, 1)
            v.wait_ge(s, n[s.name])

        def link(i):
            mark(i, dve_chain)

        def release(i, f):
            i.then_inc(side_free[f % 4], 1)
            v.wait_ge(side_free[f % 4], f // 4 + 1)

        def stt(o, i0, s, i1, op0, op1):
            return v.scalar_tensor_tensor(out=o, in0=i0, scalar=s, in1=i1, op0=op0, op1=op1)

        def per_head(ap):
            return ap.unsqueeze(2).to_broadcast([P, H, HD])

        mark(v.memset(flag[:], 0.0), flag_set)

        def x_norm(t):
            v.wait_ge(rs_ready, t + 1)
            mark(v.tensor_scalar(xn[:, t, :], x_sb[:, t, :], rs[:, t:t + 1], None, ALU.mult), xn_ready)

        def h_part(half, ks=range(KD)):
            toks = slice(256 * half, 256 * half + 256)
            for k in ks:
                v.wait_ge(hhi_ready, half * KD + k + 1)
                release(stt(h_lo[:, k, toks], side[k % 4][:, 0:256], wpre[:, k:k + 1], h_hi[:, k, toks].bitcast(F32), ALU.mult,
                            ALU.subtract), half * KD + k)

        for t in range(3):
            x_norm(t)
        h_part(0)
        x_norm(3)
        h_part(1)
        v.wait_ge(small_in, 16 * 6)

        def side_step(name, i):
            f = FILL[name, i]
            t = i
            tok = slice(t * P, (t + 1) * P) if t < NT else None
            if name == "yp":
                y_lo_part(i)
            if name == "bt":
                full(v, f)
                b = side[f % 4]
                b = b[:, 0:128].rearrange("p (t c) -> p t c", c=32)
                link(v.tensor_copy(ba_tok[:], b[:, :, 0:16]))
                release(v.tensor_tensor(ba_tok[:], b[:, :, 16:32], ba_tok[:], ALU.add), f)
                v.wait_ge(small_in, 16 * 6)
                s3 = [sp[:, q, :] for q in range(6)]
                mark(v.tensor_tensor(s3[0].rearrange("p (t h) -> p t h", h=H), ba_tok[:, :, H:2 * H],
                                     dtb[:].unsqueeze(1).to_broadcast([P, NT, H]), ALU.add), ba_args)
                mark(stt(s3[1], s3[0], -1.0, s3[0], ALU.mult, ALU.min), ba_args)
                v.wait_ge(ba_acts, 3)
                link(v.tensor_scalar(s3[3], s3[2], 2.0, None, ALU.add))
                link(v.reciprocal(s3[4], s3[3]))
                link(v.tensor_tensor(s3[1], s3[2], s3[4], ALU.mult))
                link(v.tensor_tensor(s3[2], s3[1], s3[1], ALU.mult))
                link(v.tensor_scalar(s3[3], s3[2], 1.0 / 17, None, ALU.mult))
                for c in (15, 13, 11, 9, 7, 5, 3):
                    link(stt(s3[3], s3[3], 1.0 / c, s3[2], ALU.add, ALU.mult))
                link(stt(s3[4], s3[3], 1.0, s3[1], ALU.add, ALU.mult))
                link(v.tensor_scalar(s3[5], s3[0], 0.0, None, ALU.max))
                link(stt(s3[4], s3[4], 2.0, s3[5], ALU.mult, ALU.add))
                link(v.tensor_scalar(nbeta[:], beta[:], -1.0, None, ALU.mult))
                mark(stt(g_sb[:].rearrange("p (t h) -> p t h", h=H), s3[4].rearrange("p (t h) -> p t h", h=H), -1.0,
                         alog[:].unsqueeze(1).to_broadcast([P, NT, H]), ALU.mult, ALU.mult), g_ready)
            elif name == "gm":
                freed(v, f)
                mark(v.tensor_tensor(be[:], beta[:], eg[:, 0:32], ALU.mult), be_ready)
            elif name == "cv":
                v.wait_ge(bank_copied, i + 1)
                dst = qk_dn[:, i, :] if i < 8 else v_dn[:, i - 8, :]
                c = conv_in[:, i % 2, :]
                link(v.tensor_scalar(dst, c[:, 0:S], cw[:, i, 0:1], None, ALU.mult))
                for j in range(1, 4):
                    x_ = stt(dst, c[:, j:j + S], cw[:, i, j:j + 1], dst, ALU.mult, ALU.add)
                    if j < 3:
                        link(x_)
                mark(x_, conv_done)
            elif name == "ta":
                freed(v, f + 1)
                mark(v.tensor_reduce(ssq[:, t, :], sq_tok[:].rearrange("p q (h d) -> p (q h) d", d=HD), AX.X, ALU.add),
                     ssq_ready)
            elif name == "tv":
                full(v, f)
                release(v.tensor_tensor(heads(beta_v[:, t, :]), heads(side[f % 4][:]),
                                        per_head(beta[:, t * H:(t + 1) * H]), ALU.mult), f)
            elif name == "sg" and i >= 8:
                v.wait_ge(sig_done, i + 1)
                mark(v.tensor_tensor(v_dn[:, i - 8, :], v_dn[:, i - 8, :], sig[:, i % 2, :], ALU.mult), silu_v_done)
            elif name == "ht":
                for q, src in enumerate((k_hat[:, t, :], q_tok[:, t, :])):
                    v.wait_ge(rsq_ready, 2 * t + q + 1)
                    mark(v.tensor_tensor(heads(src), heads(src), per_head(rsq[:, t, (1 - q) * H:(2 - q) * H]), ALU.mult), hat_ready)
            elif name == "tb":
                full(v, f)
                release(v.tensor_copy(qk_dn[:, 4:8, tok], side[f % 4][:].rearrange("p (m t) -> p m t", t=P)), f)
            elif name == "gr":
                d = (decay0, decay1)[t % 2]
                freed(v, FILL["dec", t])
                freed(v, FILL["dec", t] + 1)
                for q in range(2):
                    full(v, f + q)
                    for pair in range(4):
                        h = 2 * pair + q
                        x_ = stt(neg_l[:, 8 * t + h, :], side[(f + q) % 4][:, pair * P:(pair + 1) * P],
                                 nbeta[:, 8 * t + h:8 * t + h + 1], d[:, h, :], ALU.mult, ALU.mult)
                        if pair < 3:
                            link(x_)
                    release(x_, f + q)
                if t:
                    full(v, FILL["qt", t - 1] + 1)
                for q in range(2):
                    full(v, f + 2 + q)
                    release(v.tensor_tensor(qk_m[:].rearrange("p (a b) j -> p b a j", b=2)[:, q],
                                            side[(f + 2 + q) % 4][:].rearrange("p (a j) -> p a j", j=P),
                                            d[:].rearrange("p (a b) j -> p b a j", b=2)[:, q], ALU.mult), f + 2 + q)
            elif name == "qt":
                for q in range(2):
                    full(v, f + q)
                    release(v.tensor_tensor(qk_t[:, 8 * t + 4 * q:8 * t + 4 * q + 4, :],
                                            side[(f + q) % 4][:].rearrange("p (h i) -> p h i", i=P),
                                            le[:].unsqueeze(1).to_broadcast([P, 4, P]), ALU.mult), f + q)
            elif name == "bi":
                if i == 0:
                    full(v, FILL["qt", 3] + 1)
                    for b in range(4):
                        r = slice(32 * b, 32 * b + 32)
                        link(v.transpose(l_rows[r, :, :], neg_l[r, :, 32 * b:32 * b + 32].rearrange("p u j -> p j u")))
                    link(v.memset(t_rows[:], 0.0))
                    link(v.memset(t_rows[:].rearrange("p a b -> p (a b)")[:, ::33], 1.0))
                for r in range(*ROWS[i]):
                    o = prod[:, 0:r * r].rearrange("p (l j) -> p l j", j=r)
                    link(v.tensor_tensor(o, t_rows[:, 0:r, 0:r].rearrange("p j l -> p l j"),
                                         l_rows[:, 0:r, r].unsqueeze(1).to_broadcast([P, r, r]), ALU.mult))
                    link(v.tensor_reduce(t_rows[:, r, 0:r], o, AX.X, ALU.add))
            elif name == "bo":
                link(v.transpose(t_blocks[:].rearrange("p u l -> p l u"), t_rows[:].rearrange("p i l -> p l i")))
                mark(v.transpose(v_blocks[:].rearrange("p u i -> p i u"), t_rows[:]), blocks_ready)
            elif name == "ex":
                if t:
                    full(v, FILL["uw", t - 1] + 1)
                mark(block_diag(v, v_bd, v_blocks, t), vbd_ready)
            elif name == "lg":
                for q in range(2):
                    full(v, f + q)
                    release(v.tensor_tensor(gs[:, 4 * q:4 * q + 4, :], side[(f + q) % 4][:].rearrange("p (h j) -> p h j", j=P),
                                            m32[:].unsqueeze(1).to_broadcast([P, 4, P]), ALU.mult), f + q)
            elif name in ("lv", "lt"):
                m = v_bd if name == "lv" else t_bd
                for q in range(2):
                    full(v, f + q)
                    if name == "lt" and q == 0:
                        full(v, f + 1)
                    release(v.tensor_tensor(m[:, 4 * q:4 * q + 4, :], side[(f + q) % 4][:].rearrange("p (h j) -> p h j", j=P),
                                            m[:, 4 * q:4 * q + 4, :], ALU.add), f + q)
            elif name == "sa":
                freed(v, FILL["uw", t] + 1)
                full(v, f)
                if t == 0:
                    v.wait_ge(z_ready, NT)
                else:
                    full(v, FILL["ot", t - 1])
                release(v.tensor_tensor(v_new[:], u_sb[:], side[f % 4][:], ALU.subtract), f)
                full(v, f + 1)
                release(v.tensor_tensor(heads(o_acc[:]), heads(side[(f + 1) % 4][:]), per_head(eg[:, t * H:(t + 1) * H]),
                                        ALU.mult), f + 1)
            elif name == "sb":
                full(v, f)
                release(v.tensor_tensor(o_acc[:], side[f % 4][:], o_acc[:], ALU.add), f)
                full(v, f + 1)
                for q in range(2):
                    r = slice(q * HD, q * HD + HD)
                    s_ = state[r, :, r]
                    e_ = eg[r, 64 + t * H + q:64 + (t + 1) * H:2].unsqueeze(2).to_broadcast([HD, 4, HD])
                    link(v.tensor_tensor(s_, s_, e_, ALU.mult))
                    x_ = v.tensor_tensor(s_, side[(f + 1) % 4][r, 0:256].rearrange("p (a d) -> p a d", d=HD), s_, ALU.add)
                    link(x_) if q == 0 else release(x_, f + 1)
                mark(v.memset(flag[:], 0.0), o_ready)
            elif name == "on":
                v.wait_ge(osq_ready, t + 1)
                mark(v.tensor_reduce(sso[:], heads(u_sb[:]), AX.X, ALU.add), sso_ready)
            elif name == "oo":
                v.wait_ge(rso_ready, t + 1)
                mark(v.tensor_tensor(heads(o_acc[:]), heads(o_acc[:]), per_head(rso[:]), ALU.mult), on_ready)
            elif name == "a1":
                t = i // 4
                for hh in range(2):
                    full(v, f + hh)
                    b = side[(f + hh) % 4]
                    link(v.tensor_tensor(b[:, t * P:(t + 1) * P], b[:, t * P:(t + 1) * P], neg[:], ALU.add))
                    if i and hh == 0:
                        freed(v, FILL["a1", i - 1])
                        freed(v, FILL["a1", i - 1] + 1)
                    link(v.tensor_reduce(nmax[:, hh:hh + 1], b[:, 0:(t + 1) * P], AX.X, ALU.max, negate=True))
                    mark(v.tensor_scalar(nmax8[:, hh:hh + 1], nmax[:, hh:hh + 1], HD ** -0.5, None, ALU.mult), max_ready)
            elif name == "an":
                t = i // 4
                for hh in range(2):
                    freed(v, FILL["a1", i] + hh)
                    link(v.reciprocal(pinv[:, hh:hh + 1], psumr[:, hh:hh + 1]))
                    mark(v.tensor_scalar(probs[:, hh, 0:(t + 1) * P], probs[:, hh, 0:(t + 1) * P], pinv[:, hh:hh + 1], None,
                                         ALU.mult), p_ready)
            elif name == "a2":
                t = i // 4
                full(v, f + 1)
                release(v.tensor_copy(probs_t[:, 1, 0:(t + 1) * P], side[(f + 1) % 4][:, 0:(t + 1) * P]), f + 1)
            elif name == "a3":
                t, pair = i // 4, i % 4
                full(v, f)
                release(v.tensor_copy(qk_att[:, pair, t * P:(t + 1) * P], side[f % 4][:, 0:P]), f)

        def y_lo_part(j):
            v.wait_ge(yhi_ready, j + 1)
            src = (qk_dn, qk_att)[j // 2]
            mark(v.tensor_tensor(y_lo[:, 2 * j:2 * j + 2, :], src[:, 2 * (j % 2):2 * (j % 2) + 2, :],
                                 y_hi[:, 2 * j:2 * j + 2, :].bitcast(F32), ALU.subtract), ylo_ready)

        for u in range(U_IN + 1):
            for name, i in steps_at(u):
                side_step(name, i)

        y_lo_part(2)
        y_lo_part(3)
        for g in range(4):
            v.wait_ge(gates_ready, 2 * g + 2)
            v.wait_ge(unit_done, U_IN + 4 * g + 4)
            for m in range(2):
                for b, (dst, gt_) in enumerate(((m_d, gate_d), (m_a, gate_a))):
                    mark(v.tensor_tensor(dst[:, m, :], bank[g % 2 * 4 + b * 2 + m][:], gt_[:, 2 * g + m, :], ALU.mult),
                         prod_ready)
            for m in range(2):
                mark(v.tensor_tensor(m_a[:, m, :], m_a[:, m, :], m_d[:, m, :], ALU.add), m_ready)
            for m in range(2):
                v.wait_ge(mhi_ready, 2 * g + m + 1)
                mark(v.tensor_tensor(h_lo[:, 2 * g + m, :], m_a[:, m, :], h_hi[:, 2 * g + m, :].bitcast(F32),
                                     ALU.subtract), mlo_ready)

        v.wait_ge(xr_in, 16)
        v.wait_ge(pn_in, 32)
        def scaled(t, pn):
            for half in (1, 0):
                c = slice(half * 512, half * 512 + 512)
                mark(stt(tmp2[:, t % 2, c], bank[2 * t + half][:], rs1[:, t:t + 1], pn[:, c], ALU.mult, ALU.mult), y_scaled)

        def residual(t, halves):
            for half in halves:
                c = slice(half * 512, half * 512 + 512)
                mark(v.tensor_tensor(x_res[:, t, c], x_res[:, t, c], tmp2[:, t % 2, c], ALU.add), x2_ready)

        def h_norm(t):
            v.wait_ge(rs2_ready, t + 1)
            mark(v.tensor_scalar(hn[:, t, :], x_res[:, t, :], rs2[:, t:t + 1], None, ALU.mult), hn_ready)

        def h2_part(fs):
            for f in fs:
                half, k = f // KD, f % KD
                toks = slice(256 * half, 256 * half + 256)
                v.wait_ge(t2_hi, f + 1)
                mark(stt(h_lo[:, k, toks], bank[T2_BANK[f]][:, 0:256], wmlp[:, k:k + 1], h_hi[:, k, toks].bitcast(F32),
                         ALU.mult, ALU.subtract), t2_lo)

        for t in range(2):
            v.wait_ge(rs1_ready, t + 1)
            scaled(t, pn_mix)
            residual(t, (0,))
        h_norm(0)
        v.wait_ge(rs1_ready, 3)
        v.wait_ge(x2_pool, 1)
        scaled(2, pn_mix)
        h_norm(1)
        residual(2, (0, 1))
        h2_part(range(0, 4))
        v.wait_ge(rs1_ready, 4)
        v.wait_ge(x2_pool, 2)
        scaled(3, pn_mix)
        h2_part((4, 5))
        residual(3, (0, 1))
        h2_part((6, 7))
        h_norm(2)
        h_norm(3)
        h2_part(range(8, 16))

        def square(i, ms=range(4)):
            for m in ms:
                v.wait_ge(relu_done, i * 4 + (m + 1))
                v.tensor_tensor(act[:, bass.ds(i * 4 + m, 1), :].rearrange("p a s -> p (a s)"), relu[:, m, :], relu[:, m, :],
                                ALU.mult).then_inc(act_ready, 1)

        def act_lo(i, kts=range(4)):
            for kt in kts:
                v.wait_ge(ahi_ready, i * 4 + (kt + 1))
                v.tensor_tensor(a_lo[:, kt, :], act[:, bass.ds(i * 4 + kt, 1), :].rearrange("p a s -> p (a s)"),
                                a_hi[:, kt, :].bitcast(F32), ALU.subtract).then_inc(alo_ready, 1)

        with v.Fori(0, 7) as i:
            square(i)
        square(7, (0, 1))
        v.wait_ge(act_ready, 2)
        act_lo(0, (0, 1))
        square(7, (2, 3))
        v.wait_ge(act_ready, 32)
        act_lo(0, (2, 3))
        with v.Fori(1, 8) as i:
            act_lo(i)

        for t in range(NT):
            v.wait_ge(rsf_ready, t + 1)
            if t >= 2:
                v.wait_ge(y_pool, t - 1)
            scaled(t, pn_mlp)
            mark(v.tensor_tensor(y_out[:, t, 0:512], x_res[:, t, 0:512], tmp2[:, t % 2, 0:512], ALU.add), y_final)

    @block.gpsimd
    def _(g):
        n = {}

        def mark(i, s):
            n[s.name] = n.get(s.name, 0) + 1
            i.then_inc(s, 1)
            g.wait_ge(s, n[s.name])

        def link(i):
            mark(i, pool_chain)

        def select(o, op, fill, base_, step, cm):
            return g.affine_select(out=o, in_=o, compare_op=op, fill=fill, base=base_, pattern=[[step, P]],
                                   channel_multiplier=cm)

        mark(g.memset(ones[:], 1.0), ones_set)
        for c, val in ((ident, 0.0), (le, 1.0), (gt, 1.0), (neg, 0.0), (m32, 0.0), (own_block, 0.0),
                       (nhalf, -0.5), (state, 0.0)):
            link(g.memset(c[:], val))
        link(select(ident[:], ALU.not_equal, 1.0, 0, -1, 1))
        link(select(le[:], ALU.is_ge, 0.0, 0, 1, -1))
        link(select(gt[:], ALU.is_ge, 0.0, -1, -1, 1))
        link(select(neg[:], ALU.is_ge, MASKED, 0, -1, 1))
        link(g.memset(m32[0:32, 32:64], 1.0))
        link(g.memset(m32[64:96, 96:128], 1.0))
        for b in range(4):
            link(g.memset(own_block[32 * b:32 * b + 32, b:b + 1], 1.0))
        mark(g.memset(conv_in[:, :, 0:3], 0.0), consts)

        def inverse_root(dst, src, width, mean):
            link(g.tensor_scalar(src, src, mean, EPS, ALU.mult, ALU.add))
            return g.tensor_tensor(dst, src, nhalf[:, 0:width], ALU.pow)


        def split(slot, ready):
            g.wait_ge(hi_ready, ready)
            g.tensor_tensor(w_lo[:, slot, :], raw[:, slot, :], w_hi[:, slot, :].bitcast(F32),
                            ALU.subtract).then_inc(lo_ready, 1)

        def split_u(u):
            split(u % 4, u + 1)

        for t in range(NT):
            g.wait_ge(ss_ready, t + 1)
            mark(inverse_root(rs[:, t:t + 1], ss[:, t:t + 1], 1, 1.0 / D), rs_ready)
            if t in (1, 2):
                split_u(t - 1)
        split_u(2)
        split_u(3)
        g.wait_ge(bahi_ready, 1)
        mark(g.tensor_tensor(ba_w[:, :, 16:32], ba_raw[:], ba_w[:, :, 0:16].bitcast(F32), ALU.subtract), balo_ready)

        def per_head(ap):
            return ap.unsqueeze(2).to_broadcast([P, H, HD])

        def side_step(name, i):
            f = FILL[name, i]
            t = i
            if name == "sg" and i < 8:
                g.wait_ge(sig_done, i + 1)
                mark(g.tensor_tensor(qk_dn[:, i, :], qk_dn[:, i, :], sig[:, i % 2, :], ALU.mult), silu_done)
            elif name == "gk":
                g.wait_ge(g_ready, 1)
                if t >= 2:
                    full(g, FILL["dec", t - 2] + 1)
                mark(g.tensor_tensor(g_mask[:, t % 2], gt[:].unsqueeze(1).to_broadcast([P, H, P]),
                                     g_sb[:, t * H:(t + 1) * H].unsqueeze(2).to_broadcast([P, H, P]), ALU.mult), gmask_ready)
            elif name == "ta":
                g.wait_ge(ssq_ready, t + 1)
                for q in (1, 0):
                    c = slice(q * H, (q + 1) * H)
                    mark(inverse_root(rsq[:, t, c], ssq[:, t, c], H, 1.0), rsq_ready)
            elif name == "zp":
                g.wait_ge(zsig_done, t + 1)
                link(g.tensor_tensor(z_sb[:, t, :], z_sb[:, t, :], z_sig[t], ALU.mult))
                mark(g.tensor_tensor(heads(z_sb[:, t, :]), heads(z_sb[:, t, :]), dnw[:].unsqueeze(1).to_broadcast([P, H, HD]),
                                     ALU.mult), z_ready)
            elif name == "ex":
                g.wait_ge(blocks_ready, 1)
                if t:
                    freed(g, FILL["uw", t - 1] + 1)
                mark(block_diag(g, t_bd, t_blocks, t), tbd_ready)
            elif name == "kk":
                g.wait_ge(be_ready, 1)
                if t:
                    g.wait_ge(sso_ready, t)
                link(g.tensor_tensor(heads(u_sb[:]), heads(k_hat[:, t, :]), per_head(be[:, t * H:(t + 1) * H]), ALU.mult))
                mark(g.tensor_tensor(heads(k_hat[:, t, :]), heads(k_hat[:, t, :]), per_head(eg[:, 32 + t * H:32 + (t + 1) * H]),
                                     ALU.mult), kbg_ready)
            elif name == "on":
                g.wait_ge(o_ready, t + 1)
                mark(g.tensor_tensor(u_sb[:], o_acc[:], o_acc[:], ALU.mult), osq_ready)
            elif name == "oo":
                g.wait_ge(sso_ready, t + 1)
                mark(inverse_root(rso[:], sso[:], H, 1.0 / HD), rso_ready)
            elif name == "op":
                g.wait_ge(on_ready, t + 1)
                mark(g.tensor_tensor(o_acc[:], o_acc[:], z_sb[:, t, :], ALU.mult), y_ready)

        for u in range(1, U_IN + 1):
            if u < U_IN:
                split_u(u + LEAD)
            for name, i in steps_at(u):
                side_step(name, i)
        for u in range(U_IN, U_OUT - LEAD):
            split_u(u + LEAD)

        def root_y(t, s0, s):
            g.wait_ge(ssy_ready, s0 + 2 * t + 2)
            link(g.tensor_tensor(ssh[:, t:t + 1], ssy[:, 2 * t:2 * t + 1], ssy[:, 2 * t + 1:2 * t + 2], ALU.add))
            mark(inverse_root(rs1[:, t:t + 1], ssh[:, t:t + 1], 1, 1.0 / D), s)

        def root_x2(t):
            g.wait_ge(ss2_ready, t + 1)
            mark(inverse_root(rs2[:, t:t + 1], ss2[:, t:t + 1], 1, 1.0 / D), rs2_ready)

        def residual(t):
            g.wait_ge(y_scaled, 2 * t + 1)
            mark(g.tensor_tensor(x_res[:, t, 512:], x_res[:, t, 512:], tmp2[:, t % 2, 512:], ALU.add), x2_pool)

        g.wait_ge(xr_in, 16)
        root_y(0, 0, rs1_ready)
        residual(0)
        root_y(1, 0, rs1_ready)
        root_x2(0)
        residual(1)
        root_y(2, 0, rs1_ready)
        root_x2(1)
        split_u(U_OUT)
        root_y(3, 0, rs1_ready)
        split_u(U_OUT + 1)
        split_u(U_OUT + 2)
        root_x2(2)
        split_u(U_OUT + 3)
        root_x2(3)
        split_u(U_OUT + 4)
        split_u(U_OUT + 5)
        first = U_OUT + 6
        n_u = (U_ALL - first) // 4
        with g.Fori(0, n_u) as i:
            for j in range(4):
                u = first + j
                split(u % 4, i * 4 + (u + 1))
        for u in range(first + n_u * 4, U_ALL):
            split_u(u)
        for t in range(NT):
            root_y(t, 8, rsf_ready)
            g.wait_ge(y_scaled, 8 + 2 * t + 1)
            mark(g.tensor_tensor(y_out[:, t, 512:], x_res[:, t, 512:], tmp2[:, t % 2, 512:], ALU.add), y_pool)

    ctx.close()


NAMES = ["x", "pre_norm_mix", "w_in", "conv_w", "a_log", "dt_bias", "dn_norm", "w_branch_att", "w_branch_dn", "w_out",
         "post_norm_mix", "pre_norm_mlp", "w_mlp_in", "w_mlp_out", "post_norm_mlp"]


def kernel(**inputs):
    import numpy as np
    import concourse.bacc as bacc
    from concourse.bass_utils import run_bass_kernel_spmd

    nc = bacc.Bacc("TRN2", target_bir_lowering=False, num_devices=1)
    arrays, args = {}, []
    for name in NAMES:
        a = np.asarray(inputs[name])
        if name.startswith("pre_norm"):
            a = a[0].reshape(KD, P).T
        elif name == "conv_w":
            a = a[0].reshape(4, 12, P).transpose(2, 1, 0)
        a = np.ascontiguousarray(a)
        arrays["in_" + name] = a
        args.append(nc.dram_tensor("in_" + name, a.shape, mybir.dt.from_np(a.dtype), kind="ExternalInput").ap())
    args.append(nc.dram_tensor("out_0", (1, S, D), F32, kind="ExternalOutput").ap())
    program(nc, *args)
    r = run_bass_kernel_spmd(nc, [arrays], core_ids=[0])
    return r.results[0]["out_0"]
```
